# Optimizing a Trainium2 kernel written in Bass

```python
import math
import jax, jax.numpy as jnp
from jax import lax
import numpy as np

D_MODEL = 1024
BATCH = 1
SEQ = 256
DEPTH = 1

HEAD_DIM = 64
SWA_HEADS = 4
SWA_KV_HEADS = 2
SWA_WINDOW = 128
SWA_BLOCK = 128
MOBA_HEADS = 4
MOBA_BLOCK = 256
MOBA_TOPK = 3
MOBA_QCHUNK = 64
DN_HEADS = 4
DN_HEAD_DIM = 128
DN_CONV = 4
DN_CHUNK = 64
D_FF = 2816
FFN_CONV = 3

NORM_EPS = 1e-6
NEG_INF = -1e30

SWA_Q = SWA_HEADS * HEAD_DIM
SWA_KV = SWA_KV_HEADS * HEAD_DIM
MOBA_W = MOBA_HEADS * HEAD_DIM
DN_W = DN_HEADS * DN_HEAD_DIM
MIX_WIDTH = SWA_Q + MOBA_W + DN_W
IN_SPLIT_SIZES = (SWA_Q, SWA_KV, SWA_KV, MOBA_W, MOBA_W, MOBA_W, 3 * DN_W, DN_W, DN_HEADS, DN_HEADS)
IN_WIDTH = SWA_Q + 2 * SWA_KV + 3 * MOBA_W + 4 * DN_W + 2 * DN_HEADS


def rms_norm(x, w):
    xf = x.astype(jnp.float32)
    y = xf * lax.rsqrt(jnp.mean(xf * xf, axis=-1, keepdims=True) + NORM_EPS)
    return (y * w.astype(jnp.float32)).astype(x.dtype)

def l2_norm(x):
    return x * lax.rsqrt(jnp.sum(x * x, axis=-1, keepdims=True) + NORM_EPS)

def alibi_slopes():
    n = SWA_HEADS + MOBA_HEADS
    s = 2.0 ** (-8.0 * jnp.arange(1, n + 1, dtype=jnp.float32) / n)
    return s[0::2], s[1::2]

def causal_depthwise_conv(x, w):
    K = w.shape[0]
    S = x.shape[1]
    xp = jnp.pad(x, ((0, 0), (K - 1, 0), (0, 0)))
    y = xp[:, 0:S] * w[0]
    for i in range(1, K):
        y = y + xp[:, i:i + S] * w[i]
    return y

def swa_sink_attention(q, k, v, sinks, slopes):
    B, S, Hq, d = q.shape
    Hkv = k.shape[2]
    G = Hq // Hkv
    nb = S // SWA_BLOCK
    qb = q.reshape(B, nb, SWA_BLOCK, Hkv, G, d)
    kb = k.reshape(B, nb, SWA_BLOCK, Hkv, d)
    vb = v.reshape(B, nb, SWA_BLOCK, Hkv, d)

    def with_prev(t):
        prev = jnp.pad(t, ((0, 0), (1, 0), (0, 0), (0, 0), (0, 0)))[:, :-1]
        return jnp.concatenate([prev, t], axis=2)

    kk, vv = with_prev(kb), with_prev(vb)
    scores = jnp.einsum('bnqhgd,bnshd->bnhgqs', qb, kk).astype(jnp.float32) * (d ** -0.5)
    rel = jnp.arange(SWA_BLOCK)[:, None] + SWA_BLOCK - jnp.arange(2 * SWA_BLOCK)[None, :]
    kpos = (jnp.arange(nb) * SWA_BLOCK - SWA_BLOCK)[:, None] + jnp.arange(2 * SWA_BLOCK)[None, :]
    valid = ((rel >= 0) & (rel < SWA_WINDOW))[None] & (kpos >= 0)[:, None, :]
    m = slopes.astype(jnp.float32).reshape(Hkv, G)[:, :, None, None]
    scores = scores - m * rel.astype(jnp.float32)
    scores = jnp.where(valid[None, :, None, None], scores, NEG_INF)
    sink = sinks.astype(jnp.float32).reshape(Hkv, G)[:, :, None, None]
    mx = jnp.maximum(scores.max(axis=-1, keepdims=True), sink)
    p = jnp.exp(scores - mx)
    denom = p.sum(axis=-1, keepdims=True) + jnp.exp(sink - mx)
    probs = (p / denom).astype(v.dtype)
    out = jnp.einsum('bnhgqs,bnshd->bnqhgd', probs, vv)
    return out.reshape(B, S, Hq, d)

def moba_attention(q, k, v, slopes):
    B, S, H, d = q.shape
    S_pad = -(-S // MOBA_BLOCK) * MOBA_BLOCK
    pad = ((0, 0), (0, S_pad - S), (0, 0), (0, 0))
    q, k, v = jnp.pad(q, pad), jnp.pad(k, pad), jnp.pad(v, pad)
    nblk = S_pad // MOBA_BLOCK
    topk = min(MOBA_TOPK, nblk)
    kb = k.reshape(B, nblk, MOBA_BLOCK, H, d).transpose(0, 3, 1, 2, 4)
    vb = v.reshape(B, nblk, MOBA_BLOCK, H, d).transpose(0, 3, 1, 2, 4)
    k_mean = kb.astype(jnp.float32).mean(axis=3)
    nq = S_pad // MOBA_QCHUNK
    q_chunks = q.reshape(B, nq, MOBA_QCHUNK, H, d).transpose(1, 0, 3, 2, 4)
    bi = jnp.arange(B)[:, None, None, None]
    hi = jnp.arange(H)[None, :, None, None]
    m = slopes.astype(jnp.float32)[None, :, None, None]
    scale = d ** -0.5
    offs = jnp.arange(MOBA_BLOCK)

    def chunk_attend(args):
        qc, c = args
        t = c * MOBA_QCHUNK + jnp.arange(MOBA_QCHUNK)
        own = (c * MOBA_QCHUNK) // MOBA_BLOCK
        gate = jnp.einsum('bhqd,bhnd->bhqn', qc.astype(jnp.float32), k_mean)
        gate = jnp.where(jnp.arange(nblk) < own, gate, NEG_INF)
        _, idx = lax.top_k(gate, topk)
        sel_ok = idx < own
        k_sel = kb[bi, hi, idx]
        v_sel = vb[bi, hi, idx]
        s_sel = jnp.einsum('bhqd,bhqrsd->bhqrs', qc, k_sel).astype(jnp.float32) * scale
        kpos_sel = idx[..., None] * MOBA_BLOCK + offs
        s_sel = s_sel - m[..., None] * (t[:, None, None] - kpos_sel).astype(jnp.float32)
        s_sel = jnp.where(sel_ok[..., None], s_sel, NEG_INF).reshape(B, H, MOBA_QCHUNK, topk * MOBA_BLOCK)
        k_own = lax.dynamic_index_in_dim(kb, own, axis=2, keepdims=False)
        v_own = lax.dynamic_index_in_dim(vb, own, axis=2, keepdims=False)
        rel_own = t[:, None] - (own * MOBA_BLOCK + offs)[None, :]
        s_own = jnp.einsum('bhqd,bhsd->bhqs', qc, k_own).astype(jnp.float32) * scale - m * rel_own.astype(jnp.float32)
        s_own = jnp.where(rel_own >= 0, s_own, NEG_INF)
        probs = jax.nn.softmax(jnp.concatenate([s_sel, s_own], axis=-1), axis=-1).astype(v.dtype)
        p_sel = probs[..., :topk * MOBA_BLOCK].reshape(B, H, MOBA_QCHUNK, topk, MOBA_BLOCK)
        p_own = probs[..., topk * MOBA_BLOCK:]
        return (jnp.einsum('bhqrs,bhqrsd->bqhd', p_sel, v_sel)
                + jnp.einsum('bhqs,bhsd->bqhd', p_own, v_own))

    out = lax.map(chunk_attend, (q_chunks, jnp.arange(nq)))
    out = out.transpose(1, 0, 2, 3, 4).reshape(B, S_pad, H, d)
    return out[:, :S]

def gated_delta_rule(q, k, v, g, beta):
    B, S, H, dk = q.shape
    dv = v.shape[-1]
    C = DN_CHUNK
    nc = S // C

    def chunks(t):
        t = t.reshape((B, nc, C, H) + t.shape[3:])
        return jnp.moveaxis(t, 3, 1)

    q = chunks(q) * (dk ** -0.5)
    k = chunks(k)
    v = chunks(v)
    g = jnp.cumsum(chunks(g), axis=-1)
    beta = chunks(beta)
    causal = jnp.tril(jnp.ones((C, C), dtype=bool))
    strict = jnp.tril(jnp.ones((C, C), dtype=bool), -1)
    gdiff = g[..., :, None] - g[..., None, :]
    decay = jnp.where(causal, jnp.exp(jnp.where(causal, gdiff, 0.0)), 0.0)
    k_beta = k * beta[..., None]
    L = jnp.where(strict, jnp.einsum('bhnid,bhnjd->bhnij', k_beta, k) * decay, 0.0)
    rhs = jnp.concatenate([v * beta[..., None], k_beta * jnp.exp(g)[..., None]], axis=-1)
    sol = lax.linalg.triangular_solve(L + jnp.eye(C, dtype=L.dtype), rhs, left_side=True,
                                      lower=True, unit_diagonal=True)
    u, w = sol[..., :dv], sol[..., dv:]
    a_intra = jnp.einsum('bhnid,bhnjd->bhnij', q, k) * decay
    q_dec = q * jnp.exp(g)[..., None]
    g_last = g[..., -1]
    k_dec = k * jnp.exp(g_last[..., None] - g)[..., None]

    def step(state, xs):
        w_c, u_c, qd_c, a_c, kd_c, gl_c = xs
        v_new = u_c - jnp.einsum('bhcd,bhde->bhce', w_c, state)
        o = jnp.einsum('bhcd,bhde->bhce', qd_c, state) + jnp.einsum('bhij,bhje->bhie', a_c, v_new)
        state = state * jnp.exp(gl_c)[..., None, None] + jnp.einsum('bhcd,bhce->bhde', kd_c, v_new)
        return state, o

    xs = (jnp.moveaxis(w, 2, 0), jnp.moveaxis(u, 2, 0), jnp.moveaxis(q_dec, 2, 0),
          jnp.moveaxis(a_intra, 2, 0), jnp.moveaxis(k_dec, 2, 0), jnp.moveaxis(g_last, 2, 0))
    state0 = jnp.zeros((B, H, dk, dv), jnp.float32)
    _, o = lax.scan(step, state0, xs)
    return o.transpose(1, 0, 3, 2, 4).reshape(B, S, H, dv)

def hybrid_token_mixer(h, w_in, swa_sinks, dn_conv_w, dn_a_log, dn_dt_bias, dn_norm, w_out,
                       slopes_swa, slopes_moba):
    B, S, _ = h.shape
    proj = h @ w_in
    split_at = np.cumsum(IN_SPLIT_SIZES)[:-1].tolist()
    qa, ka, va, qb, kb, vb, qkv_c, z_c, b_c, a_c = jnp.split(proj, split_at, axis=-1)
    o_a = swa_sink_attention(qa.reshape(B, S, SWA_HEADS, HEAD_DIM),
                             ka.reshape(B, S, SWA_KV_HEADS, HEAD_DIM),
                             va.reshape(B, S, SWA_KV_HEADS, HEAD_DIM), swa_sinks, slopes_swa)
    o_b = moba_attention(qb.reshape(B, S, MOBA_HEADS, HEAD_DIM), kb.reshape(B, S, MOBA_HEADS, HEAD_DIM),
                         vb.reshape(B, S, MOBA_HEADS, HEAD_DIM), slopes_moba)
    qkv_c = jax.nn.silu(causal_depthwise_conv(qkv_c, dn_conv_w)).astype(jnp.float32)
    qc, kc, vc = jnp.split(qkv_c, 3, axis=-1)
    qc = l2_norm(qc.reshape(B, S, DN_HEADS, DN_HEAD_DIM))
    kc = l2_norm(kc.reshape(B, S, DN_HEADS, DN_HEAD_DIM))
    vc = vc.reshape(B, S, DN_HEADS, DN_HEAD_DIM)
    beta = jax.nn.sigmoid(b_c.astype(jnp.float32))
    g = -jnp.exp(dn_a_log.astype(jnp.float32)) * jax.nn.softplus(a_c.astype(jnp.float32) + dn_dt_bias.astype(jnp.float32))
    o_c = gated_delta_rule(qc, kc, vc, g, beta)
    o_c = rms_norm(o_c, dn_norm) * jax.nn.silu(z_c.astype(jnp.float32).reshape(B, S, DN_HEADS, DN_HEAD_DIM))
    mixed = jnp.concatenate([o_a.reshape(B, S, SWA_Q), o_b.reshape(B, S, MOBA_W),
                             o_c.reshape(B, S, DN_W).astype(h.dtype)], axis=-1)
    return mixed @ w_out

def conv_glu_ffn(h, w_up, conv_w, conv_b, w_down):
    u = causal_depthwise_conv(h @ w_up, conv_w) + conv_b
    gate, up = jnp.split(u, 2, axis=-1)
    return (jax.nn.gelu(gate, approximate=True) * up) @ w_down

def first_inputs(seed: int = 0) -> dict:
    key = jax.random.key(seed)
    ks = jax.random.split(key, 16)
    f32 = jnp.float32

    def nrm(k, shape, scale):
        return jax.random.normal(k, shape, f32) * scale

    dt = jnp.exp(jax.random.uniform(ks[6], (DEPTH, DN_HEADS), f32)
                 * (math.log(0.1) - math.log(0.001)) + math.log(0.001))
    return {
        'x': nrm(ks[0], (BATCH, SEQ, D_MODEL), 1.0),
        'mix_pre_norm': 1.0 + nrm(ks[1], (DEPTH, D_MODEL), 0.05),
        'w_in': nrm(ks[2], (DEPTH, D_MODEL, IN_WIDTH), D_MODEL ** -0.5),
        'swa_sinks': nrm(ks[3], (DEPTH, SWA_HEADS), 0.5),
        'dn_conv_w': nrm(ks[4], (DEPTH, DN_CONV, 3 * DN_W), DN_CONV ** -0.5),
        'dn_a_log': jnp.log(jax.random.uniform(ks[5], (DEPTH, DN_HEADS), f32, 1.0, 16.0)),
        'dn_dt_bias': dt + jnp.log(-jnp.expm1(-dt)),
        'dn_norm': 1.0 + nrm(ks[7], (DEPTH, DN_HEAD_DIM), 0.05),
        'w_out': nrm(ks[8], (DEPTH, MIX_WIDTH, D_MODEL), MIX_WIDTH ** -0.5),
        'mix_post_norm': 1.0 + nrm(ks[9], (DEPTH, D_MODEL), 0.05),
        'ffn_pre_norm': 1.0 + nrm(ks[10], (DEPTH, D_MODEL), 0.05),
        'w_up': nrm(ks[11], (DEPTH, D_MODEL, 2 * D_FF), D_MODEL ** -0.5),
        'ffn_conv_w': nrm(ks[12], (DEPTH, FFN_CONV, 2 * D_FF), FFN_CONV ** -0.5),
        'ffn_conv_b': nrm(ks[13], (DEPTH, 2 * D_FF), 0.02),
        'w_down': nrm(ks[14], (DEPTH, D_FF, D_MODEL), D_FF ** -0.5),
        'ffn_post_norm': 1.0 + nrm(ks[15], (DEPTH, D_MODEL), 0.05),
    }

def first_block(x, mix_pre_norm, w_in, swa_sinks, dn_conv_w, dn_a_log, dn_dt_bias, dn_norm, w_out,
              mix_post_norm, ffn_pre_norm, w_up, ffn_conv_w, ffn_conv_b, w_down, ffn_post_norm):
    slopes_swa, slopes_moba = alibi_slopes()
    for l in range(DEPTH):
        h = rms_norm(x, mix_pre_norm[l])
        mix = hybrid_token_mixer(h, w_in[l], swa_sinks[l], dn_conv_w[l], dn_a_log[l], dn_dt_bias[l],
                                 dn_norm[l], w_out[l], slopes_swa, slopes_moba)
        x = x + rms_norm(mix, mix_post_norm[l])
        h = rms_norm(x, ffn_pre_norm[l])
        x = x + rms_norm(conv_glu_ffn(h, w_up[l], ffn_conv_w[l], ffn_conv_b[l], w_down[l]), ffn_post_norm[l])
    return x


DEPTH_2 = 2

CHUNK = 64
N_A = DEPTH_2 // 2
N_B = DEPTH_2 - N_A
GMLP_BLOCK = 128
GATE_DIM = 2 * D_MODEL
A_GROUPS = 8
A_GROUP_DIM = GATE_DIM // A_GROUPS
B_HEADS = 8
QK_NOPE = 128
QK_ROPE = 64
V_HEAD = 128
Q_LORA = 384
KV_LORA = 256
ROPE_THETA = 10000.0
Q_BLOCK = 128
D_FF_2 = 4 * D_MODEL
EPS = 1e-6


def rmsnorm(x, g):
    xf = x.astype(jnp.float32)
    y = xf * lax.rsqrt(jnp.mean(xf * xf, axis=-1, keepdims=True) + EPS)
    return (y * g.astype(jnp.float32)).astype(x.dtype)

def layernorm(x, g, b):
    xf = x.astype(jnp.float32)
    mu = jnp.mean(xf, axis=-1, keepdims=True)
    var = jnp.mean(jnp.square(xf - mu), axis=-1, keepdims=True)
    y = (xf - mu) * lax.rsqrt(var + EPS)
    return (y * g.astype(jnp.float32) + b.astype(jnp.float32)).astype(x.dtype)

def rope_angles(positions):
    inv_freq = ROPE_THETA ** (-jnp.arange(0, QK_ROPE, 2, dtype=jnp.float32) / QK_ROPE)
    return positions.astype(jnp.float32)[..., None] * inv_freq

def apply_rope(x, ang):
    xf = x.astype(jnp.float32)
    x1, x2 = jnp.split(xf, 2, axis=-1)
    c, s = jnp.cos(ang), jnp.sin(ang)
    return jnp.concatenate([x1 * c - x2 * s, x2 * c + x1 * s], axis=-1).astype(x.dtype)

def chunk_mask(q_idx, k_idx):
    return (k_idx[None, :] // CHUNK) <= (q_idx[:, None] // CHUNK)

def gmlp_mixer(hn, w_in, ln_g, ln_b, w_s, b_s, w_out):
    B, S, _ = hn.shape
    z = jax.nn.gelu(hn @ w_in, approximate=False)
    u, v = jnp.split(z, 2, axis=-1)
    v = layernorm(v, ln_g, ln_b)
    nb = S // GMLP_BLOCK
    vb = v.reshape(B, nb, GMLP_BLOCK, A_GROUPS, A_GROUP_DIM)
    idx = jnp.arange(GMLP_BLOCK)
    ws = jnp.where(chunk_mask(idx, idx)[None], w_s, jnp.zeros_like(w_s))
    sv = jnp.einsum('gij,bnjgc->bnigc', ws, vb) + b_s.T[None, None, :, :, None]
    return (u * sv.reshape(B, S, GATE_DIM)) @ w_out

def shared_latent_kv(h, positions, src_g, w_kv_a, kv_a_g, w_kv_b):
    B, S, _ = h.shape
    hn = rmsnorm(h, src_g)
    ckv = hn @ w_kv_a
    c_kv, k_pe = ckv[..., :KV_LORA], ckv[..., KV_LORA:]
    c_kv = rmsnorm(c_kv, kv_a_g)
    kv = (c_kv @ w_kv_b).reshape(B, S, B_HEADS, QK_NOPE + V_HEAD)
    k_nope, v = kv[..., :QK_NOPE], kv[..., QK_NOPE:]
    k_pe = apply_rope(k_pe, rope_angles(positions))
    return k_nope, k_pe, v

def chunk_causal_mla_attention(q_nope, q_pe, k_nope, k_pe, v):
    B, S, H, _ = q_nope.shape
    nb = S // Q_BLOCK
    qn = q_nope.reshape(B, nb, Q_BLOCK, H, QK_NOPE).transpose(1, 0, 2, 3, 4)
    qp = q_pe.reshape(B, nb, Q_BLOCK, H, QK_ROPE).transpose(1, 0, 2, 3, 4)
    k_idx = jnp.arange(S)
    scale = (QK_NOPE + QK_ROPE) ** -0.5

    def one_block(args):
        qn_b, qp_b, i = args
        s = (jnp.einsum('bqhd,bkhd->bhqk', qn_b, k_nope).astype(jnp.float32)
             + jnp.einsum('bqhd,bkd->bhqk', qp_b, k_pe).astype(jnp.float32)) * scale
        q_idx = i * Q_BLOCK + jnp.arange(Q_BLOCK)
        s = jnp.where(chunk_mask(q_idx, k_idx)[None, None], s, jnp.finfo(jnp.float32).min)
        p = jax.nn.softmax(s, axis=-1).astype(v.dtype)
        return jnp.einsum('bhqk,bkhd->bqhd', p, v)

    out = lax.map(one_block, (qn, qp, jnp.arange(nb)))
    return out.transpose(1, 0, 2, 3, 4).reshape(B, S, H, V_HEAD)

def mla_mixer(hn, kv, positions, w_q_a, q_g, w_q_b, w_o):
    B, S, _ = hn.shape
    k_nope, k_pe, v = kv
    cq = rmsnorm(hn @ w_q_a, q_g)
    q = (cq @ w_q_b).reshape(B, S, B_HEADS, QK_NOPE + QK_ROPE)
    q_nope = q[..., :QK_NOPE]
    q_pe = apply_rope(q[..., QK_NOPE:], rope_angles(positions)[:, :, None, :])
    o = chunk_causal_mla_attention(q_nope, q_pe, k_nope, k_pe, v)
    return o.reshape(B, S, B_HEADS * V_HEAD) @ w_o

def sq_relu_mlp(hn, w1, w2):
    return jnp.square(jax.nn.relu(hn @ w1)) @ w2

def second_inputs(seed: int = 0) -> dict:
    key = jax.random.key(seed)
    ks = jax.random.split(key, 24)

    def nrm(k, shape, fan_in, mult=1.0):
        return jax.random.normal(k, shape, jnp.float32) * (mult * fan_in ** -0.5)

    def gain(k, shape):
        return 1.0 + 0.05 * jax.random.normal(k, shape, jnp.float32)

    x = jax.random.normal(ks[0], (BATCH, SEQ, D_MODEL), jnp.float32)
    offset = jax.random.randint(ks[1], (BATCH, 1), 0, 4096, dtype=jnp.int32)
    positions = offset + jnp.arange(SEQ, dtype=jnp.int32)[None, :]
    return {
        "x": x,
        "positions": positions,
        "norm_mix_g": gain(ks[2], (DEPTH_2, D_MODEL)),
        "norm_mlp_g": gain(ks[3], (DEPTH_2, D_MODEL)),
        "a_w_in": nrm(ks[4], (N_A, D_MODEL, 2 * GATE_DIM), D_MODEL),
        "a_ln_v_g": gain(ks[5], (N_A, GATE_DIM)),
        "a_ln_v_b": 0.02 * jax.random.normal(ks[6], (N_A, GATE_DIM), jnp.float32),
        "a_w_s": nrm(ks[7], (N_A, A_GROUPS, GMLP_BLOCK, GMLP_BLOCK), GMLP_BLOCK, 0.5),
        "a_b_s": 1.0 + 0.1 * jax.random.normal(ks[8], (N_A, A_GROUPS, GMLP_BLOCK), jnp.float32),
        "a_w_out": nrm(ks[9], (N_A, GATE_DIM, D_MODEL), GATE_DIM),
        "b_w_q_a": nrm(ks[10], (N_B, D_MODEL, Q_LORA), D_MODEL),
        "b_q_norm_g": gain(ks[11], (N_B, Q_LORA)),
        "b_w_q_b": nrm(ks[12], (N_B, Q_LORA, B_HEADS * (QK_NOPE + QK_ROPE)), Q_LORA),
        "b_w_o": nrm(ks[13], (N_B, B_HEADS * V_HEAD, D_MODEL), B_HEADS * V_HEAD),
        "kv_src_norm_g": gain(ks[14], (D_MODEL,)),
        "kv_w_a": nrm(ks[15], (D_MODEL, KV_LORA + QK_ROPE), D_MODEL),
        "kv_a_norm_g": gain(ks[16], (KV_LORA,)),
        "kv_w_b": nrm(ks[17], (KV_LORA, B_HEADS * (QK_NOPE + V_HEAD)), KV_LORA),
        "mlp_w1": nrm(ks[18], (DEPTH_2, D_MODEL, D_FF_2), D_MODEL),
        "mlp_w2": nrm(ks[19], (DEPTH_2, D_FF_2, D_MODEL), D_FF_2, 0.5),
        "final_norm_g": gain(ks[20], (D_MODEL,)),
    }

def second_block(x, positions, norm_mix_g, norm_mlp_g, a_w_in, a_ln_v_g, a_ln_v_b, a_w_s,
              a_b_s, a_w_out, b_w_q_a, b_q_norm_g, b_w_q_b, b_w_o, kv_src_norm_g, kv_w_a,
              kv_a_norm_g, kv_w_b, mlp_w1, mlp_w2, final_norm_g):
    h = x
    kv = None
    for l in range(DEPTH_2):
        hn = rmsnorm(h, norm_mix_g[l])
        if l < N_A:
            h = h + gmlp_mixer(hn, a_w_in[l], a_ln_v_g[l], a_ln_v_b[l], a_w_s[l],
                               a_b_s[l], a_w_out[l])
        else:
            j = l - N_A
            h = h + mla_mixer(hn, kv, positions, b_w_q_a[j], b_q_norm_g[j], b_w_q_b[j], b_w_o[j])
        h = h + sq_relu_mlp(rmsnorm(h, norm_mlp_g[l]), mlp_w1[l], mlp_w2[l])
        if l == N_A - 1:
            kv = shared_latent_kv(h, positions, kv_src_norm_g, kv_w_a, kv_a_norm_g, kv_w_b)
    return rmsnorm(h, final_norm_g)


def setup_inputs(seed=0):
    out = dict(first_inputs(seed))
    for name, value in second_inputs(seed + 1).items():
        if name != "x":
            out[name + "_2"] = value
    return out


def reference(
    x, mix_pre_norm, w_in, swa_sinks, dn_conv_w, dn_a_log, dn_dt_bias, dn_norm, w_out,
    mix_post_norm, ffn_pre_norm, w_up, ffn_conv_w, ffn_conv_b, w_down, ffn_post_norm,
    positions_2, norm_mix_g_2, norm_mlp_g_2, a_w_in_2, a_ln_v_g_2, a_ln_v_b_2, a_w_s_2, a_b_s_2,
    a_w_out_2, b_w_q_a_2, b_q_norm_g_2, b_w_q_b_2, b_w_o_2, kv_src_norm_g_2, kv_w_a_2,
    kv_a_norm_g_2, kv_w_b_2, mlp_w1_2, mlp_w2_2, final_norm_g_2,
):
    x = first_block(
        x, mix_pre_norm, w_in, swa_sinks, dn_conv_w, dn_a_log, dn_dt_bias, dn_norm, w_out,
        mix_post_norm, ffn_pre_norm, w_up, ffn_conv_w, ffn_conv_b, w_down, ffn_post_norm,
    )
    return second_block(
        x, positions_2, norm_mix_g_2, norm_mlp_g_2, a_w_in_2, a_ln_v_g_2, a_ln_v_b_2, a_w_s_2,
        a_b_s_2, a_w_out_2, b_w_q_a_2, b_q_norm_g_2, b_w_q_b_2, b_w_o_2, kv_src_norm_g_2,
        kv_w_a_2, kv_a_norm_g_2, kv_w_b_2, mlp_w1_2, mlp_w2_2, final_norm_g_2,
    )


_drawn_inputs = setup_inputs


def setup_inputs(seed=0):
    import zlib

    import numpy as np

    out = dict(_drawn_inputs(seed))
    spreads = {}
    factors = {'ffn_conv_b': 3.253,
     'a_ln_v_g_2': 7.473,
     'a_ln_v_b_2': 8.0,
     'b_q_norm_g_2': 8.0,
     'kv_src_norm_g_2': 7.498,
     'kv_a_norm_g_2': 6.149}
    for name, (base, spread) in spreads.items():
        noise = np.random.default_rng([zlib.crc32(name.encode()), seed]).standard_normal(out[name].shape)
        drawn = base * np.exp(spread * noise) if base else spread * noise
        out[name] = __import__('jax').numpy.asarray(drawn.astype(out[name].dtype))
    for name, factor in factors.items():
        out[name] = (out[name] * factor).astype(out[name].dtype)
    return out
```

```python
import math
from contextlib import ExitStack

import concourse.bass as bass
from concourse import mybir

ALU = mybir.AluOpType
ACT = mybir.ActivationFunctionType
F32 = mybir.dt.float32
F32R = mybir.dt.float32r
I32 = mybir.dt.int32
AX_X = mybir.AxisListType.X

P = 128
S = 256
TB = S // P
D = 1024
KT = D // P
UNIT = 2048
UC = UNIT // KT
PAIR = UC // P
RAW = 3
SPL = 3
PERIOD = 6
EPS = 1e-6
ROOM = 17300
HD = 64
NH = 4
DN = 128
CH = 64
G8 = TB * NH
LEVELS = 6
MH = 8
ROPE = 64
FF1 = 2816
FT1 = FF1 // P
GATE = 2048
TWO_PI = 2.0 * math.pi
C1 = 6.28125
C2 = 0.0019350051879882812
C3 = TWO_PI - C1 - C2
MAGIC = 12582912.0

G_MIX, G_FFN, G_MIX2, G_MLP2, G_SRC = 0, 8, 16, 32, 48
CONV_D, G_Q, G_KV = 56, 104, 107
CONV_F = 109
NPAR = CONV_F + 4 * 2 * FT1

T_ID, T_TRI, T_BLK, T_NEG, T_LOW, T_LEV = 0, 128, 256, 384, 512, 640
T_MLA = T_LEV + LEVELS * P
T_INV, T_SGN = T_MLA + S, T_MLA + S + 1
T_ALL = T_SGN + 1


def build(nc, I, out, stages):
    ctx = ExitStack()
    with ctx:
        def sb(name, shape, dt=F32):
            return ctx.enter_context(nc.sbuf_tensor(name, shape, dt))

        def sem(name):
            return ctx.enter_context(nc.semaphore(name))

        raw = sb("raw", [P, RAW, UNIT])
        w_hi = sb("w_hi", [P, SPL, UNIT], F32R)
        w_lo = sb("w_lo", [P, SPL, UNIT], F32R)
        X = sb("X", [P, TB, D])
        XN = sb("XN", [P, TB, D])
        hT_hi = sb("hT_hi", [P, KT, S], F32R)
        hT_lo = sb("hT_lo", [P, KT, S], F32R)
        act_tmp = sb("act_tmp", [P, 4, 512])
        act_f = sb("act_f", [P, 3, 512])
        act_hi = sb("act_hi", [P, 3, 512], F32R)
        act_lo = sb("act_lo", [P, 3, 512], F32R)
        par = sb("par", [P, NPAR])
        ident = sb("ident", [P, P])
        rows = sb("rows", [P, D])
        stat = sb("stat", [P, 16])
        mhalf = sb("mhalf", [P, 16])
        ps = [ctx.enter_context(nc.psum_tensor(f"ps{b}", [P, 512], F32)) for b in range(8)]
        W, ACC = ps[:4], ps[4:]

        units = []
        first_unit = {}

        def cols(w, c0, n=UC, at=0, of=UC):
            k = w.shape[0] // P
            src = w[:, c0:c0 + n].rearrange("(k p) n -> p k n", p=P)
            return (k * of, lambda slot: (raw[:, slot, 0:k * of].rearrange("p (k n) -> p k n", k=k)[:, :, at:at + n], src))

        def rws(w, r0, n=UC):
            src = w[r0:r0 + n, :].rearrange("(k p) n -> p k n", p=P)
            return (n // P * D, lambda slot: (raw[:, slot, 0:n // P * D].rearrange("p (k n) -> p k n", n=D), src))

        def unit(*parts):
            units.append((max(p[0] for p in parts), [p[1] for p in parts]))

        w_in, w_out, w_up, w_down = I["w_in"][0], I["w_out"][0], I["w_up"][0], I["w_down"][0]
        a_in, a_out = I["a_w_in_2"][0], I["a_w_out_2"][0]
        q_a, q_b, w_o = I["b_w_q_a_2"][0], I["b_w_q_b_2"][0], I["b_w_o_2"][0]
        kv_a, kv_b = I["kv_w_a_2"], I["kv_w_b_2"]
        for st in stages:
            first_unit[st] = len(units)
            if st == "mix":
                for c0 in (512, 768, 1024, 256):
                    unit(cols(w_in, c0))
                unit(cols(w_in, 0, HD, 0), cols(w_in, 2 * HD, HD, HD), cols(w_in, HD, HD, 2 * HD), cols(w_in, 3 * HD, HD, 3 * HD))
                unit(cols(w_in, 3328, 8, 0, 8))
                for c0 in (1280, 1536, 1792, 2048, 2304, 2560, 2816, 3072):
                    unit(cols(w_in, c0))
                for r in range(4):
                    unit(rws(w_out, r * UC))
            elif st == "ffn":
                for j in range(FT1 // PAIR):
                    unit(cols(w_up, j * UC))
                    unit(cols(w_up, FF1 + j * UC))
                    if j:
                        unit(rws(w_down, (j - 1) * UC))
                unit(rws(w_down, FF1 - UC))
            elif st == "gmlp":
                for j in range(8):
                    unit(cols(a_in, GATE + j * UC))
                for j in range(8):
                    unit(cols(a_in, j * UC))
                    if j:
                        unit(rws(a_out, (j - 1) * UC))
                unit(rws(a_out, 7 * UC))
            elif st in ("mlp0", "mlp1"):
                l = int(st[3])
                for j in range(16):
                    unit(cols(I["mlp_w1_2"][l], j * UC))
                    if j:
                        unit(rws(I["mlp_w2_2"][l], (j - 1) * UC))
                unit(rws(I["mlp_w2_2"][l], 15 * UC))
            elif st == "mla":
                unit(cols(kv_a, 0))
                unit(cols(kv_a, 256, 64, 0), cols(kv_a, 256, 64, 64),
                     cols(kv_a, 288, 32, 128), cols(kv_a, 256, 32, 160),
                     cols(kv_a, 288, 32, 192), cols(kv_a, 256, 32, 224))
                unit(cols(q_a, 0))
                unit(cols(q_a, 256, 128, 0, 128))
                for g in range(2):
                    unit(cols(kv_b, g * 1024, 1024, 0, 1024))
                for g in range(4):
                    c = g * 384
                    unit(cols(q_b, c, P, 0, 512), cols(q_b, c + 192, P, P, 512),
                         cols(q_b, c + 128, ROPE, 256, 512), cols(q_b, c + 320, ROPE, 320, 512),
                         cols(q_b, c + 160, 32, 384, 512), cols(q_b, c + 128, 32, 416, 512),
                         cols(q_b, c + 352, 32, 448, 512), cols(q_b, c + 320, 32, 480, 512))
                for r in range(4):
                    unit(rws(w_o, r * UC))
        NU = len(units)
        landed = [sem(f"landed{s}") for s in range(RAW)]
        landed_at = [16 * sum(len(units[v][1]) for v in range(u % RAW, u + 1, RAW)) for u in range(NU)]
        hi_ready = sem("hi_ready")
        lo_ready = sem("lo_ready")
        unit_used = sem("unit_used")

        def load(sp, u, i=0, src=None):
            if u >= RAW:
                sp.wait_ge(lo_ready, u - RAW + 1 + PERIOD * i)
            for part in units[u][1]:
                dst, view = part(u % RAW)
                sp.dma_start(dst, view if src is None else src).then_inc(landed[u % RAW], 16)

        def split_hi(act, u, i=0):
            if u >= NU:
                return
            n, s, r = units[u][0], u % SPL, u % RAW
            act.wait_ge(landed[r], landed_at[u] + 16 * (PERIOD // RAW) * i)
            if u >= SPL:
                act.wait_ge(unit_used, u - SPL + 1 + PERIOD * i)
            nc.scalar.activation(w_hi[:, s, 0:n], raw[:, r, 0:n], ACT.Copy).then_inc(hi_ready, 1)

        def split_lo(dve, u, i=0):
            if u >= NU:
                return
            n, s, r = units[u][0], u % SPL, u % RAW
            dve.wait_ge(hi_ready, u + 1 + PERIOD * i)
            nc.vector.tensor_tensor(w_lo[:, s, 0:n], raw[:, r, 0:n], w_hi[:, s, 0:n].bitcast(F32),
                                    ALU.subtract).then_inc(lo_ready, 1)

        def weights(u, k):
            n = units[u][0]
            return [w[:, u % SPL, 0:n].rearrange("p (k n) -> p k n", k=k) for w in (w_hi, w_lo)]

        def mm3(o, a, b, start, stop):
            nc.tensor.matmul(o, a[0], b[0], start=start, stop=False)
            nc.tensor.matmul(o, a[1], b[0], start=False, stop=False)
            return nc.tensor.matmul(o, a[0], b[1], start=False, stop=stop)

        HT = (hT_hi, hT_lo)

        def features(o, w, c, act, k, wait=None):
            for t in range(k):
                if wait is not None:
                    wait(t)
                mm = mm3(o, [x[:, t, c] for x in w], [x[:, t, :] for x in act], t == 0, t == k - 1)
            return mm

        def tokens(o, w, c, act, k, tb, wait=None):
            for t in range(k):
                if wait is not None:
                    wait(t)
                mm = mm3(o, [x[:, t, tb * P:(tb + 1) * P] for x in act], [x[:, t, c] for x in w], t == 0, t == k - 1)
            return mm

        x_in = [sem(f"x_in{tb}") for tb in range(TB)]
        par_in = sem("par_in")
        id_in = sem("id_in")
        g_in, g_tr, g_ok = sem("g_in"), sem("g_tr"), sem("g_ok")
        filled = sem("filled")
        par_tr = sem("par_tr")
        par_ok = sem("par_ok")
        pstage = act_f[:, 0, 0:384].rearrange("p (t f) -> p t f", t=3)

        def rowsof(v):
            return v.rearrange("a (f p) -> (a f) p", p=P)

        def start_sync(sp):
            xv = I["x"][0].rearrange("(b p) d -> p b d", p=P)
            for tb in range(TB):
                sp.dma_start(X[:, tb, :], xv[:, tb, :]).then_inc(x_in[tb], 16)

        def start_act_dmas(act):
            act.dma_start(ident[:], I["table"][:, T_ID:T_ID + P]).then_inc(id_in, 16)
            act.dma_start(pstage[0:KT, 0, :], rowsof(I["mix_pre_norm"])).then_inc(g_in, 16)

        def params_sync(sp):
            r = KT
            for v in (I["ffn_pre_norm"], I["norm_mix_g_2"], I["norm_mlp_g_2"],
                      I["kv_src_norm_g_2"].rearrange("(a d) -> a d", a=1), I["dn_conv_w"][0], I["b_q_norm_g_2"],
                      I["kv_a_norm_g_2"].rearrange("(a d) -> a d", a=1)):
                n = v.shape[0] * v.shape[1] // P
                sp.dma_start(pstage[r:r + n, 0, :], rowsof(v)).then_inc(par_in, 16)
                r += n
            taps = rowsof(I["ffn_conv_w"][0])
            sp.dma_start(pstage[0:4 * FT1, 1, :], taps[0:4 * FT1, :]).then_inc(par_in, 16)
            sp.dma_start(pstage[0:2 * FT1, 2, :], taps[4 * FT1:6 * FT1, :]).then_inc(par_in, 16)
            sp.dma_start(pstage[2 * FT1:4 * FT1, 2, :], rowsof(I["ffn_conv_b"])).then_inc(par_in, 16)

        def start_dve(dve):
            nc.vector.memset(mhalf[:], -0.5).then_inc(filled, 1)

        def start_pe(pe):
            pe.wait_ge(par_in, 16 * 10)
            pe.wait_ge(g_ok, 1)
            pe.transpose(W[3][:, 0:109], pstage[0:109, 0, :], ident[0:109, 0:109])
            pe.transpose(W[3][:, 109:197], pstage[0:88, 1, :], ident[0:88, 0:88])
            pe.transpose(W[3][:, 197:285], pstage[0:88, 2, :], ident[0:88, 0:88]).then_inc(par_tr, 1)

        def gain_pe(pe):
            pe.wait_ge(id_in, 16)
            pe.wait_ge(g_in, 16)
            pe.transpose(W[3][:, 0:KT], pstage[0:KT, 0, :], ident[0:KT, 0:KT]).then_inc(g_tr, 1)

        def gain_act(act):
            act.wait_ge(g_tr, 1)
            nc.scalar.copy(par[:, 0:KT], W[3][:, 0:KT]).then_inc(g_ok, 1)

        def start_act(act):
            act.wait_ge(par_tr, 1)
            nc.scalar.copy(par[:, KT:NPAR], W[3][:, KT:NPAR]).then_inc(par_ok, 1)
            act.wait_ge(par_ok, 1)

        def warm(pe, n):
            for k in range(n):
                nc.tensor.matmul(W[2][:, 0:P], ident[:], ident[:], start=True, stop=True)

        x_done = sem("x_done")
        n_sq, n_ms, n_rstd, n_xa, n_xv = sem("n_sq"), sem("n_ms"), sem("n_rstd"), sem("n_xa"), sem("n_xv")
        n_tr, n_hi, n_lo = sem("n_tr"), sem("n_hi"), sem("n_lo")

        def half(b):
            return X[:, b // 2, b % 2 * 512:b % 2 * 512 + 512]

        def turned(t):
            return ACC[t % 4][:, t // 4 * S:(t // 4 + 1) * S]

        def norm_act(act, n, gain, evac=True):
            for b in range(4):
                if n == 0:
                    act.wait_ge(x_in[b // 2], 16)
                else:
                    act.wait_ge(x_done, 4 * (n - 1) + b + 1)
                nc.scalar.activation(act_tmp[:, b, :], half(b), ACT.Square, scale=D ** -0.5,
                                     accum_out=stat[:, b:b + 1]).then_inc(n_sq, 1)
                if evac and b > 1:
                    act.wait_ge(n_rstd, TB * n + b - 1)
                    nc.scalar.mul(XN[:, b - 2, 0:512], X[:, b - 2, 0:512], stat[:, 4 + b:5 + b]).then_inc(n_xa, 1)
            if evac:
                if n == 0:
                    gain_act(act)
                    split_hi(act, 0)
                norm_hi(act, n, gain)

        def norm_hi(act, n, gain, again=0):
            if n == 0:
                act.wait_ge(g_ok, 1)
            elif n == 1:
                act.wait_ge(par_ok, 1)
            for t in range(KT):
                if t < 4 and not again:
                    act.wait_ge(n_tr, 4 * n + t + 1)
                if t >= 4:
                    act.wait_ge(n_lo, n_hi_count[n] + 8 * again + t - 3)
                nc.scalar.mul(hT_hi[:, t, :], turned(t), par[:, gain + t:gain + t + 1]).then_inc(n_hi, 1)

        def norm_dve(dve, n, gain, close, evac=True):
            for b in range(4):
                close(b)
                if b % 2:
                    dve.wait_ge(n_sq, 4 * n + b + 1)
                    nc.vector.scalar_tensor_tensor(stat[:, 4 + b // 2:5 + b // 2], stat[:, b - 1:b], EPS,
                                                   stat[:, b:b + 1], ALU.add, ALU.add).then_inc(n_ms, 1)
                elif b and evac:
                    norm_rows(dve, n, 0)
            if evac:
                norm_rows(dve, n, 1)
                if n == 0:
                    split_lo(dve, 0)
                    dve.wait_ge(g_ok, 1)
                norm_lo(dve, n, gain)

        def norm_rows(dve, n, tb):
            dve.wait_ge(n_rstd, TB * n + tb + 1)
            nc.vector.tensor_scalar(XN[:, tb, 512:D], X[:, tb, 512:D], stat[:, 6 + tb:7 + tb], None, ALU.mult).then_inc(n_xv, 1)

        def norm_lo(dve, n, gain, again=0):
            base = n_hi_count[n] + 8 * again
            for t in range(KT):
                dve.wait_ge(n_hi, base + t + 1)
                nc.vector.scalar_tensor_tensor(hT_lo[:, t, :], turned(t), par[:, gain + t:gain + t + 1],
                                               hT_hi[:, t, :].bitcast(F32), ALU.mult, ALU.subtract).then_inc(n_lo, 1)

        def norm_pool(pool, n):
            if n == 0:
                pool.wait_ge(filled, 1)
            for tb in range(TB):
                pool.wait_ge(n_ms, TB * n + tb + 1)
                nc.gpsimd.tensor_tensor(stat[:, 6 + tb:7 + tb], stat[:, 4 + tb:5 + tb], mhalf[:, 0:1],
                                        ALU.pow).then_inc(n_rstd, 1)

        def norm_pe(pe, n, after_post):
            if n == 0:
                pe.wait_ge(id_in, 16)
            for tb in range(TB):
                pe.wait_ge(n_xa, TB * n + tb + 1)
                pe.wait_ge(n_xv, TB * n + tb + 1)
                for t in (0, 4, 1, 5, 2, 6, 3, 7):
                    if n and tb == 0 and 0 < t < 4 and not after_post:
                        pe.wait_ge(x_done, 4 * (n - 1) + t + 1)
                    mm = pe.transpose(turned(t)[:, tb * P:(tb + 1) * P], XN[:, tb, t * P:(t + 1) * P], ident[:])
                    if tb and t >= 4:
                        mm.then_inc(n_tr, 1)

        def h_ready(pe, n, again=0):
            base = n_hi_count[n] + 8 * again
            return lambda t: pe.wait_ge(n_lo, base + t + 1)

        rows_in = sem("rows_in")
        r_sq, r_ms, r_rstd, r_t = sem("r_sq"), sem("r_ms"), sem("r_rstd"), sem("r_t")

        acc_done = sem("acc_done")

        def sum_done(eng, n, b, last_unit):
            if b < 3:
                eng.wait_ge(acc_done, 3 * n + b + 1)
            else:
                eng.wait_ge(unit_used, last_unit + 1)

        def res_dve(dve, n, last_unit):
            def close(b):
                sum_done(dve, n, b, last_unit)
                nc.vector.tensor_tensor(half(b), ACC[b][:], half(b), ALU.add).then_inc(x_done, 1)
            return close

        def post_act(act, n, last_unit):
            for b in range(4):
                sum_done(act, n, b, last_unit)
                nc.scalar.activation(act_tmp[:, b, :], ACC[b][:], ACT.Square, scale=D ** -0.5,
                                     accum_out=stat[:, 8 + b:9 + b]).then_inc(r_sq, 1)

        def post_pool(pool, q):
            for tb in range(TB):
                pool.wait_ge(r_ms, TB * q + tb + 1)
                nc.gpsimd.tensor_tensor(stat[:, 14 + tb:15 + tb], stat[:, 12 + tb:13 + tb], mhalf[:, 0:1],
                                        ALU.pow).then_inc(r_rstd, 1)

        def post_dve(dve, q):
            dve.wait_ge(rows_in, 16 * (q + 1))
            for b in range(4):
                dve.wait_ge(r_sq, 4 * q + b + 1)
                nc.vector.tensor_tensor(act_tmp[:, b, :], ACC[b][:], rows[:, b % 2 * 512:b % 2 * 512 + 512],
                                        ALU.mult).then_inc(r_t, 1)
                if b % 2:
                    nc.vector.scalar_tensor_tensor(stat[:, 12 + b // 2:13 + b // 2], stat[:, 7 + b:8 + b], EPS,
                                                   stat[:, 8 + b:9 + b], ALU.add, ALU.add).then_inc(r_ms, 1)

            def close(b):
                dve.wait_ge(r_rstd, TB * q + b // 2 + 1)
                dve.wait_ge(r_t, 4 * q + b + 1)
                nc.vector.scalar_tensor_tensor(half(b), act_tmp[:, b, :], stat[:, 14 + b // 2:15 + b // 2], half(b),
                                               ALU.mult, ALU.add).then_inc(x_done, 1)
            return close

        def rows_load(pool, k, v):
            if k:
                pool.wait_ge(r_t, 4 * k)
            pool.dma_start(rows[:], v.partition_broadcast(P)).then_inc(rows_in, 16)

        def tiles2(x, m):
            return x[:, m, :].rearrange("p (t s) -> p t s", t=PAIR)

        def up(o, u, wait=None):
            w = weights(u, KT)
            for t in range(PAIR):
                mm = features(o[:, t * S:(t + 1) * S], w, slice(t * P, (t + 1) * P), HT, KT, wait if t == 0 else None)
            mm.then_inc(unit_used, 1)

        def down(u, acts, first=False, last=False):
            w = weights(u, PAIR)
            order = [(t, tb) for t in range(PAIR) for tb in range(TB)]
            for t, tb in sorted(order, key=lambda x: x[::-1]) if last else order:
                for h in range(2):
                    mm = mm3(ACC[2 * tb + h][:], [x[:, t, tb * P:(tb + 1) * P] for x in acts],
                             [x[:, t, h * 512:(h + 1) * 512] for x in w], first and t == 0, last and t == PAIR - 1)
                    if last and t == PAIR - 1 and 2 * tb + h < 3:
                        mm.then_inc(acc_done, 1)
            mm.then_inc(unit_used, 1)

        class Pass:
            def __init__(self, st, pairs, u0):
                self.pairs, self.u0 = pairs, u0
                self.t = sem(st + "_t")
                if st == "ffn":
                    self.c1 = sem(st + "_c1")
                    self.c2 = sem(st + "_c2")
                    self.g = sem(st + "_g")
                self.f = sem(st + "_f")
                self.hi = sem(st + "_hi")
                self.lo = sem(st + "_lo")

        def each_pair(eng, f, per, step, u_of):
            bodies = (f.pairs - 2) // per
            looped = bodies if bodies > 2 else 0
            step(1, 1, u_of(1), 0)
            if looped:
                with eng.Fori(0, looped) as i:
                    for m in range(per):
                        step(i * per + (m + 2), (m + 2) % per, u_of(m + 2), i)
            for j in range(per * looped + 2, f.pairs):
                step(j, j % per, u_of(j), 0)

        def plain_pe(pe, f, per, wait, last_wait=None):
            def step(j, m, u, i):
                pe.wait_ge(lo_ready, u + 1 + i * PERIOD)
                pe.wait_ge(f.t, j)
                up(W[m], u)
                pe.wait_ge(f.lo, j)
                pe.wait_ge(lo_ready, u + 2 + i * PERIOD)
                down(u + 1, (tiles2(act_hi, (m - 1) % per), tiles2(act_lo, (m - 1) % per)), first=isinstance(j, int) and j == 1)
            each_pair(pe, f, per, step, lambda j: f.u0 + 2 * j - 1)
            u = f.u0 + 2 * f.pairs - 1
            m = (f.pairs - 1) % per
            pe.wait_ge(f.lo, f.pairs)
            pe.wait_ge(lo_ready, u + 1)
            down(u, (tiles2(act_hi, m), tiles2(act_lo, m)), last=True)

        def plain_act(act, f, per, func, extra=None):
            def step(j, m, u, i):
                first = isinstance(j, int) and j == 0
                act.wait_ge(unit_used, u + 1 + i * PERIOD)
                if not first:
                    act.wait_ge(f.f, j)
                nc.scalar.activation(act_tmp[:, m, :], W[m][:], func).then_inc(f.t, 1)
                last = isinstance(j, int) and j == f.pairs - 1
                if not last:
                    split_hi(act, u + 3, i)
                act.wait_ge(f.f, j + 1)
                nc.scalar.copy(act_hi[:, m, :], act_f[:, m, :]).then_inc(f.hi, 1)
                if last:
                    split_hi(act, u + 3, i)
                if not first:
                    split_hi(act, u + 4, i)
                if extra is not None and isinstance(j, int):
                    extra(act, j)
            step(0, 0, f.u0, 0)
            each_pair(act, f, per, step, lambda j: f.u0 + 2 * j - 1)

        def plain_dve(dve, f, per, factor, extra=None):
            def step(j, m, u, i):
                first = isinstance(j, int) and j == 0
                dve.wait_ge(f.t, j + 1)
                if not first:
                    dve.wait_ge(f.hi, j)
                nc.vector.tensor_tensor(act_f[:, m, :], act_tmp[:, m, :], factor(j, m), ALU.mult).then_inc(f.f, 1)
                last = isinstance(j, int) and j == f.pairs - 1
                if not last:
                    split_lo(dve, u + 3, i)
                dve.wait_ge(f.hi, j + 1)
                nc.vector.tensor_tensor(act_lo[:, m, :], act_f[:, m, :], act_hi[:, m, :].bitcast(F32),
                                        ALU.subtract).then_inc(f.lo, 1)
                if last:
                    split_lo(dve, u + 3, i)
                if not first and u != f.u0 + 2 * f.pairs - 3:
                    split_lo(dve, u + 4, i)
                if extra is not None and isinstance(j, int):
                    extra(dve, j)
            step(0, 0, f.u0, 0)
            each_pair(dve, f, per, step, lambda j: f.u0 + 2 * j - 1)

        def mlp_sync(sp, f, w1, w2):
            load(sp, f.u0)

            def step(j, m, u, i):
                load(sp, u, i, w1[:, bass.ds(j * UC, UC)].rearrange("(k p) n -> p k n", p=P))
                load(sp, u + 1, i, w2[bass.ds((j - 1) * UC, UC), :].rearrange("(k p) n -> p k n", p=P))
            each_pair(sp, f, 3, step, lambda j: f.u0 + 2 * j - 1)
            load(sp, f.u0 + 2 * f.pairs - 1)

        def conv_taps(j, half, t, tap):
            c = CONV_F + tap * 2 * FT1 + half * FT1 + t
            return par[:, c:c + 1] if isinstance(j, int) and j == 0 else par[:, bass.ds(j * PAIR + c, 1)]

        def ffn_pe(pe, f, ready):
            def step(j, m, u, i):
                first = isinstance(j, int) and j == 0
                pe.wait_ge(lo_ready, u + 1 + i * PERIOD)
                if not first:
                    pe.wait_ge(f.c2, j * 4 - 2)
                up(W[2 * m], u, ready if first else None)
                pe.wait_ge(lo_ready, u + 2 + i * PERIOD)
                up(W[2 * m + 1], u + 1)
                if not first:
                    pe.wait_ge(f.lo, j)
                    pe.wait_ge(lo_ready, u + 3 + i * PERIOD)
                    down(u + 2, (tiles2(act_hi, 1 - m), tiles2(act_lo, 1 - m)), first=isinstance(j, int) and j == 1)
            step(0, 0, f.u0, 0)
            each_pair(pe, f, 2, step, lambda j: f.u0 + 3 * j - 1)
            u, m = f.u0 + 3 * f.pairs - 1, (f.pairs - 1) % 2
            pe.wait_ge(f.lo, f.pairs)
            pe.wait_ge(lo_ready, u + 1)
            down(u, (tiles2(act_hi, m), tiles2(act_lo, m)), last=True)

        def ffn_act(act, f):
            def step(j, m, u, i):
                first = isinstance(j, int) and j == 0
                for half in range(2):
                    act.wait_ge(unit_used, u + half + 1 + i * PERIOD)
                    if not first and half == 0:
                        act.wait_ge(f.f, j)
                    for t in range(PAIR):
                        nc.scalar.activation(act_tmp[:, 2 * m + half, t * S:(t + 1) * S],
                                             W[2 * m + half][:, t * S:(t + 1) * S], ACT.Identity,
                                             bias=conv_taps(j, half, t, 3), scale=conv_taps(j, half, t, 2)).then_inc(f.t, 1)
                    last = isinstance(j, int) and j == f.pairs - 1
                    if not (half and last):
                        split_hi(act, u + half + 3, i)
                act.wait_ge(f.c2, j * 4 + 2)
                nc.scalar.activation(act_tmp[:, 2 * m, :], act_tmp[:, 2 * m, :], ACT.Gelu_apprx_tanh).then_inc(f.g, 1)
                act.wait_ge(f.f, j + 1)
                nc.scalar.copy(act_hi[:, m, :], act_f[:, m, :]).then_inc(f.hi, 1)
                if last:
                    split_hi(act, u + 4, i)
                if not first:
                    split_hi(act, u + 5, i)
            act.wait_ge(par_ok, 1)
            step(0, 0, f.u0, 0)
            each_pair(act, f, 2, step, lambda j: f.u0 + 3 * j - 1)

        def ffn_dve(dve, f):
            def step(j, m, u, i):
                first = isinstance(j, int) and j == 0
                for half in range(2):
                    bank, y = W[2 * m + half], act_tmp[:, 2 * m + half, :]
                    for back, done in ((1, f.c1), (2, f.c2)):
                        for t in range(PAIR):
                            if back == 1:
                                dve.wait_ge(f.t, j * 4 + (2 * half + 2))
                            else:
                                dve.wait_ge(f.c1, j * 4 + (2 * half + t + 1))
                            ys = y[:, t * S + back:(t + 1) * S]
                            nc.vector.scalar_tensor_tensor(ys, bank[:, t * S:(t + 1) * S - back],
                                                           conv_taps(j, half, t, 2 - back), ys, ALU.mult,
                                                           ALU.add).then_inc(done, 1)
                    last = isinstance(j, int) and j == f.pairs - 1
                    if not (half and last):
                        split_lo(dve, u + half + 3, i)
                dve.wait_ge(f.g, j + 1)
                dve.wait_ge(f.c2, j * 4 + 4)
                if not first:
                    dve.wait_ge(f.hi, j)
                nc.vector.tensor_tensor(act_f[:, m, :], act_tmp[:, 2 * m, :], act_tmp[:, 2 * m + 1, :],
                                        ALU.mult).then_inc(f.f, 1)
                dve.wait_ge(f.hi, j + 1)
                nc.vector.tensor_tensor(act_lo[:, m, :], act_f[:, m, :], act_hi[:, m, :].bitcast(F32),
                                        ALU.subtract).then_inc(f.lo, 1)
                if last:
                    split_lo(dve, u + 4, i)
                if not first and u != f.u0 + 3 * f.pairs - 4:
                    split_lo(dve, u + 5, i)
            step(0, 0, f.u0, 0)
            each_pair(dve, f, 2, step, lambda j: f.u0 + 3 * j - 1)

        def ffn_sync(sp, f):
            load(sp, f.u0)
            load(sp, f.u0 + 1)

            def step(j, m, u, i):
                load(sp, u, i, w_up[:, bass.ds(j * UC, UC)].rearrange("(k p) n -> p k n", p=P))
                load(sp, u + 1, i, w_up[:, bass.ds(j * UC + FF1, UC)].rearrange("(k p) n -> p k n", p=P))
                load(sp, u + 2, i, w_down[bass.ds((j - 1) * UC, UC), :].rearrange("(k p) n -> p k n", p=P))
            each_pair(sp, f, 2, step, lambda j: f.u0 + 3 * j - 1)
            load(sp, f.u0 + 3 * f.pairs - 1)

        o_g, o_out = sem("o_g"), sem("o_out")

        def final_dve(dve, n, q):
            dve.wait_ge(rows_in, 16 * (q + 1))
            for tb in range(TB):
                dve.wait_ge(n_rstd, TB * n + tb + 1)
                ot = act_tmp[:, 2 * tb:2 * tb + 2, :].rearrange("p a b -> p (a b)")
                nc.vector.scalar_tensor_tensor(ot, X[:, tb, :], stat[:, 6 + tb:7 + tb], rows[:], ALU.mult, ALU.mult).then_inc(o_g, 1)

        def final_sync(sp):
            ov = out[0].rearrange("(b p) d -> p b d", p=P)
            for tb in range(TB):
                sp.wait_ge(o_g, tb + 1)
                sp.dma_start(ov[:, tb, :], act_tmp[:, 2 * tb:2 * tb + 2, :].rearrange("p a b -> p (a b)")).then_inc(o_out, 16)
            sp.wait_ge(o_out, 32)

        union = sb("union", [P, ROOM])

        def cutter():
            at = [0]

            def cut(*shape, p=P):
                n = math.prod(shape)
                v = union[0:p, at[0]:at[0] + n]
                at[0] += n
                assert at[0] <= ROOM, at[0]
                names = "abc"[:len(shape)]
                if len(shape) > 1:
                    v = v.rearrange(f"p ({' '.join(names)}) -> p {' '.join(names)}", **dict(zip(names, shape)))
                return v
            return cut

        cut = cutter()
        GG = 8
        GT = GATE // P
        gv = cut(TB, GATE)
        svT = cut(GT, S)
        svC = cut(GT, P)
        wsr, wsT = cut(GG, P), cut(GG, P)
        bsr = cut(GG, P)
        ones = cut(P)
        lnr = cut(P)
        lnp = cut(2 * GT)
        bnst = cut(TB, GG, 6)
        mv = cut(TB, 2)
        vrs = cut(TB, 1)
        s_in = sem("s_in")
        s_wt, s_ws, s_wz, s_rs, s_sc = sem("s_wt"), sem("s_ws"), sem("s_wz"), sem("s_rs"), sem("s_sc")
        s_g, s_bn, s_mv, s_ve, s_vr = sem("s_g"), sem("s_bn"), sem("s_mv"), sem("s_ve"), sem("s_vr")
        s_ln, s_mix, s_cp = sem("s_ln"), sem("s_mix"), sem("s_cp")

        def gmlp_pool(pool, n):
            pool.wait_ge(s_mv, TB)
            nc.gpsimd.tensor_scalar(vrs[:, :, 0], mv[:, :, 1], EPS, None, ALU.add).then_inc(s_ve, 1)
            pool.wait_ge(s_ve, 1)
            nc.gpsimd.tensor_tensor(vrs[:, :, 0], vrs[:, :, 0], mhalf[:, 0:TB], ALU.pow).then_inc(s_vr, 1)

        def gmlp_loads(pool, n):
            pool.wait_ge(x_done, 4 * (n - 1))
            pool.dma_start(wsr, I["a_w_s_2"][0].rearrange("g i j -> i g j")).then_inc(s_in, 16)
            pool.dma_start(lnr[0:GT, :], rowsof(I["a_ln_v_g_2"])).then_inc(s_in, 16)
            pool.dma_start(lnr[GT:2 * GT, :], rowsof(I["a_ln_v_b_2"])).then_inc(s_in, 16)
            pool.dma_start(bsr, I["a_b_s_2"][0].partition_broadcast(P)).then_inc(s_in, 16)

        def gmlp_ws_pe(pe, n):
            pe.wait_ge(s_in, 64)
            pe.wait_ge(n_lo, n_hi_count[n] + KT)
            for g in range(GG):
                pe.transpose(ACC[g // 4][:, g % 4 * P:(g % 4 + 1) * P], wsr[:, g, :], ident[:])
            pe.transpose(ACC[2][:, 0:2 * GT], lnr[0:2 * GT, :], ident[0:2 * GT, 0:2 * GT]).then_inc(s_wt, 1)

        def gmlp_ws_dve(dve, n):
            dve.wait_ge(x_done, 4 * (n - 1))
            nc.vector.memset(ones, 1.0).then_inc(s_ws, 1)
            dve.wait_ge(s_wt, 1)
            nc.vector.tensor_copy(lnp, ACC[2][:, 0:2 * GT]).then_inc(s_ws, 1)
            for b in range(2):
                nc.vector.tensor_copy(wsT[:, 4 * b:4 * b + 4, :], ACC[b][:].rearrange("p (g i) -> p g i", g=4)).then_inc(s_ws, 1)
            dve.wait_ge(s_ws, 4)
            nc.vector.memset(wsT[CH:P, :, 0:CH], 0.0).then_inc(s_wz, 1)

        def gmlp_rows_pe(pe):
            pe.wait_ge(s_wz, 1)
            for b in range(2):
                nc.tensor.matmul(ACC[2 + b][:], ones, wsT[:, 4 * b:4 * b + 4, :], start=True, stop=True).then_inc(s_rs, 1)

        def gmlp_rows_dve(dve):
            for t in range(GT):
                g = t // 2
                dve.wait_ge(s_rs, g // 4 + 1)
                nc.vector.scalar_tensor_tensor(svC[:, t, :], ACC[2 + g // 4][:, g % 4 * P:(g % 4 + 1) * P],
                                               lnp[:, GT + t:GT + t + 1], bsr[:, g, :], ALU.mult, ALU.add).then_inc(s_sc, 1)

        def gmlp_pe(pe, n, f, ready):
            u0 = first_unit["gmlp"]
            for j in range(8):
                u = u0 + j
                pe.wait_ge(lo_ready, u + 1)
                if j >= 4:
                    pe.wait_ge(s_g, j - 3)
                w = weights(u, KT)
                for tb in range(TB):
                    mm = tokens(W[j % 4][:, tb * UC:(tb + 1) * UC], w, slice(0, UC), HT, KT, tb,
                                ready if j == tb == 0 else None)
                mm.then_inc(unit_used, 1)
                if j == 0:
                    gmlp_ws_pe(pe, n)
                elif j == 3:
                    gmlp_rows_pe(pe)
            pe.wait_ge(lo_ready, f.u0 + 1)
            pe.wait_ge(s_g, 5)
            up(W[0], f.u0)
            for p in range(8):
                if p == 0:
                    pe.wait_ge(s_sc, GT)
                    pe.wait_ge(s_ln, TB)
                if p >= 4:
                    pe.wait_ge(s_cp, 2 * (p - 3))
                for t in range(PAIR):
                    for tb in range(TB):
                        c = (2 * p + t) * P
                        mm = nc.tensor.matmul(ACC[p % 4][:, t * S + tb * P:t * S + (tb + 1) * P], gv[:, tb, c:c + P],
                                              wsT[:, p, :], start=True, stop=True)
                mm.then_inc(s_mix, 1)
            pe.wait_ge(s_cp, GT)
            plain_pe(pe, f, 3, ready)

        def gmlp_act(act, n, f):
            u0 = first_unit["gmlp"]
            for j in range(8):
                act.wait_ge(unit_used, u0 + j + 1)
                nc.scalar.activation(gv[:, :, j * UC:(j + 1) * UC], W[j % 4][:].rearrange("p (b c) -> p b c", b=TB),
                                     ACT.Gelu).then_inc(s_g, 1)
                split_hi(act, u0 + j + 3)
            plain_act(act, f, 3, ACT.Gelu)

        def gmlp_dve(dve, n, f):
            u0 = first_unit["gmlp"]
            for j in range(8):
                dve.wait_ge(s_g, j + 1)
                for tb in range(TB):
                    nc.vector.bn_stats(bnst[:, tb, j, :], gv[:, tb, j * UC:(j + 1) * UC]).then_inc(s_bn, 1)
                if j == 7:
                    dve.wait_ge(s_bn, 16)
                    for tb in range(TB):
                        nc.vector.bn_aggr(mv[:, tb, :], bnst[:, tb, :, :].rearrange("p a b -> p (a b)")).then_inc(s_mv, 1)
                split_lo(dve, u0 + j + 3)
                if j == 1:
                    gmlp_ws_dve(dve, n)
                elif j == 4:
                    gmlp_rows_dve(dve)
            dve.wait_ge(s_vr, 1)
            for tb in range(TB):
                nc.vector.tensor_scalar(gv[:, tb, :], gv[:, tb, :], mv[:, tb, 0:1], vrs[:, tb, :], ALU.subtract,
                                        ALU.mult).then_inc(s_ln, 1)
            for t in range(GT):
                dve.wait_ge(s_mix, t // 2 + 1)
                if t == 0:
                    dve.wait_ge(s_sc, GT)
                nc.vector.scalar_tensor_tensor(svT[:, t, :].rearrange("p (b i) -> p b i", b=TB),
                                               ACC[t // 2 % 4][:, t % 2 * S:(t % 2 + 1) * S].rearrange("p (b i) -> p b i", b=TB),
                                               lnp[:, t:t + 1], svC[:, t, :].unsqueeze(1).to_broadcast([P, TB, P]),
                                               ALU.mult, ALU.add).then_inc(s_cp, 1)
            dve.wait_ge(s_cp, GT)
            plain_dve(dve, f, 3, lambda j, m: svT[:, bass.ds(j * 2, 2) if not isinstance(j, int) else slice(2 * j, 2 * j + 2), :].rearrange("p t s -> p (t s)"))

        a_s, a_b, a_c, a_nm, a_e = sem("a_s"), sem("a_b"), sem("a_c"), sem("a_nm"), sem("a_e")
        a_sd, a_rd, a_p, a_t, a_pt = sem("a_sd"), sem("a_rd"), sem("a_p"), sem("a_t"), sem("a_pt")
        a_o, a_oh, a_ol = sem("a_o"), sem("a_oh"), sem("a_ol")
        a_mx = sb("a_mx", [P, 2, 24])
        PT = act_f[:].rearrange("p a b -> p (a b)")[:, 0:2 * NH * P].rearrange("p (k h q) -> p k h q", k=2, h=NH)

        class Group:
            def __init__(self, tb, q, k, v, scale, bias, sink, where, ahead):
                self.tb, self.q, self.k, self.v = tb, q, k, v
                self.scale, self.bias, self.sink, self.where = scale, bias, sink, where
                self.n = (tb + 1) * P
                self.ahead = ahead
                self.g = None

        groups = []

        def add_group(gr):
            gr.g = len(groups)
            gr.nb0 = sum(x.tb + 1 for x in groups)
            gr.nc0 = sum(1 + (x.sink is not None) for x in groups)
            gr.ne0 = sum(NH + (x.sink is not None) for x in groups)
            groups.append(gr)
            return gr

        def probs(gr):
            return act_tmp[:].rearrange("p a b -> p (a b)")[:, gr.g % 2 * 1024:gr.g % 2 * 1024 + NH * gr.n].rearrange(
                "p (h k) -> p h k", h=NH)

        def heads_of(gr, b):
            return (0, 4) if gr.tb == 0 else (2 * b, 2 * b + 2)

        def score_bank(gr, b):
            return W[2 * (gr.g % 2) + b] if gr.ahead == 2 else W[2 + b]

        def at_scores(pe, gr):
            if gr.g >= gr.ahead:
                pe.wait_ge(a_b, groups[gr.g - gr.ahead + 1].nb0)
            for b in range(gr.tb + 1):
                h0, h1 = heads_of(gr, b)
                for h in range(h0, h1):
                    o = score_bank(gr, b)[:, (h - h0) * gr.n:(h - h0 + 1) * gr.n]
                    qs, ks = gr.q(h), gr.k(h)
                    for m in range(len(qs)):
                        mm = nc.tensor.matmul(o, qs[m], ks[m], start=m == 0, stop=m == len(qs) - 1)
                mm.then_inc(a_s, 1)

        def at_turn(pe, gr):
            pe.wait_ge(a_p, gr.g + 1)
            pe.wait_ge(a_pt, gr.nb0)
            pr = probs(gr)
            for kb in range(gr.tb + 1):
                for h in range(NH):
                    tr = pe.transpose(ACC[kb][:, h * P:(h + 1) * P], pr[:, h, kb * P:(kb + 1) * P], ident[:])
                tr.then_inc(a_t, 1)

        def at_out(pe, gr):
            pe.wait_ge(a_pt, gr.nb0 + gr.tb + 1)
            if gr.g >= 2:
                pe.wait_ge(a_ol, gr.g - 1)
            for h in range(NH):
                o = gr.where["psum"](ACC[2 + gr.g % 2], h)
                for kb in range(gr.tb + 1):
                    mm = nc.tensor.matmul(o, gr.v(h, kb), PT[:, kb, h, :], start=kb == 0, stop=kb == gr.tb)
            mm.then_inc(a_o, 1)

        def at_max(dve, gr):
            pr, m = probs(gr), a_mx[:, gr.g % 2, :]
            if gr.g >= 2:
                dve.wait_ge(a_t, groups[gr.g - 1].nb0)
            for b in range(gr.tb + 1):
                h0, h1 = heads_of(gr, b)
                dve.wait_ge(a_s, gr.nb0 + b + 1)
                bank = score_bank(gr, b)[:].rearrange("p (h k) -> p h k", k=gr.n)
                nc.vector.scalar_tensor_tensor(pr[:, h0:h1, :], bank, gr.scale, gr.bias(h0, h1), ALU.mult,
                                               ALU.add).then_inc(a_b, 1)
            dve.wait_ge(a_b, gr.nb0 + gr.tb + 1)
            nc.vector.tensor_reduce(m[:, 0:4], pr, AX_X, ALU.max).then_inc(a_c, 1)
            dve.wait_ge(a_c, gr.nc0 + 1)
            if gr.sink is None:
                nc.vector.tensor_scalar(m[:, 4:8], m[:, 0:4], -1.0, None, ALU.mult).then_inc(a_nm, 1)
            else:
                nc.vector.tensor_tensor(m[:, 20:24], m[:, 0:4], gr.sink, ALU.max).then_inc(a_c, 1)
                dve.wait_ge(a_c, gr.nc0 + 2)
                nc.vector.tensor_tensor(m[:, 12:16], gr.sink, m[:, 20:24], ALU.subtract)
                nc.vector.tensor_scalar(m[:, 4:8], m[:, 20:24], -1.0, None, ALU.mult).then_inc(a_nm, 1)

        def at_exp(act, gr):
            pr, m = probs(gr), a_mx[:, gr.g % 2, :]
            act.wait_ge(a_nm, gr.g + 1)
            for h in range(NH):
                nc.scalar.activation(pr[:, h, :], pr[:, h, :], ACT.Exp, bias=m[:, 4 + h:5 + h],
                                     accum_out=m[:, 8 + h:9 + h]).then_inc(a_e, 1)
            if gr.sink is not None:
                nc.scalar.activation(m[:, 12:16], m[:, 12:16], ACT.Exp).then_inc(a_e, 1)

        def at_norm(dve, gr):
            pr, m = probs(gr), a_mx[:, gr.g % 2, :]
            dve.wait_ge(a_e, gr.ne0 + NH + (gr.sink is not None))
            if gr.sink is not None:
                nc.vector.tensor_tensor(m[:, 16:20], m[:, 8:12], m[:, 12:16], ALU.add).then_inc(a_sd, 1)
                dve.wait_ge(a_sd, gr.g + 1)
                nc.vector.reciprocal(m[:, 20:24], m[:, 16:20]).then_inc(a_rd, 1)
            else:
                nc.vector.reciprocal(m[:, 20:24], m[:, 8:12]).then_inc(a_rd, 1)
            dve.wait_ge(a_rd, gr.g + 1)
            nc.vector.tensor_tensor(pr, pr, m[:, 20:24].unsqueeze(2).to_broadcast([P, NH, gr.n]), ALU.mult).then_inc(a_p, 1)

        def at_copy(act, gr):
            if gr.g >= 1:
                act.wait_ge(a_o, gr.g)
            for kb in range(gr.tb + 1):
                act.wait_ge(a_t, gr.nb0 + kb + 1)
                nc.scalar.copy(PT[:, kb, :, :], ACC[kb][:].rearrange("p (h q) -> p h q", h=NH)).then_inc(a_pt, 1)

        def at_hi(act, gr):
            act.wait_ge(a_o, gr.g + 1)
            dst, src = gr.where["out"](hT_hi, ACC[2 + gr.g % 2])
            nc.scalar.copy(dst, src).then_inc(a_oh, 1)

        def at_lo(dve, gr):
            dve.wait_ge(a_oh, gr.g + 1 - (NH if "mix" in stages else 0))
            hi, src = gr.where["out"](hT_hi, ACC[2 + gr.g % 2])
            lo, _ = gr.where["out"](hT_lo, ACC[2 + gr.g % 2])
            nc.vector.tensor_tensor(lo, src, hi.bitcast(F32), ALU.subtract).then_inc(a_ol, 1)

        def at_keep(act, gr, x):
            act.wait_ge(a_o, gr.g + 1)
            dst, src = gr.where["out"](x, ACC[2 + gr.g % 2])
            nc.scalar.copy(dst, src).then_inc(a_ol, 1)

        def attend_pe(pe, gs):
            for k, gr in enumerate(gs):
                if k:
                    at_turn(pe, gr)
                if k + 2 < len(gs):
                    at_scores(pe, gs[k + 2])
                at_out(pe, gr)

        def attend_act(act, gs, split):
            at_copy(act, gs[0])
            split(0)
            at_exp(act, gs[2])
            at_hi(act, gs[0])
            at_copy(act, gs[1])
            at_exp(act, gs[3])
            split(1)
            at_hi(act, gs[1])
            for gr in gs[2:]:
                at_copy(act, gr)
                at_hi(act, gr)

        def attend_dve(dve, gs, split):
            at_norm(dve, gs[1])
            split(0)
            at_max(dve, gs[2])
            at_lo(dve, gs[0])
            at_max(dve, gs[3])
            at_norm(dve, gs[2])
            split(1)
            at_lo(dve, gs[1])
            at_norm(dve, gs[3])
            at_lo(dve, gs[2])
            at_lo(dve, gs[3])

        cut = cutter()
        knT = cut(MH, S)
        kpe = cut(2, S)
        mv_v = cut(TB, MH * P)
        qnT = cut(MH, S)
        qpe = cut(MH // 2, S)
        cn = cut(TB, 256)
        cqn = cut(TB, 384)
        mtab = cut(S + 2)
        mpos, ang, kt_, kc_, r1, r2, cosT, sinT = (cut(S) for _ in range(8))
        ropet = cut(4, S)
        lst = cut(20)
        cT = [x[:].rearrange("p a b -> p (a b)").rearrange("p (t s) -> p t s", s=S)[:, 0:2, :] for x in (act_hi, act_lo)]
        cqT = [x[:].rearrange("p a b -> p (a b)").rearrange("p (t s) -> p t s", s=S)[:, 2:5, :] for x in (act_hi, act_lo)]
        m_in, m_ch = sem("m_in"), sem("m_ch")
        m_cs = sem("m_cs")
        m_sq, m_p1, m_rs, m_cn, m_ct, m_ch2, m_cl = (sem(f"m_{x}") for x in ("sq", "p1", "rs", "cn", "ct", "chi", "clo"))
        m_kz = sem("m_kz")
        m_kp, m_ev, m_rp, m_rq = sem("m_kp"), sem("m_ev"), sem("m_rp"), sem("m_rq")
        posi = ropet[:, 0, :].bitcast(I32)

        def mla_groups():
            out = []
            for hg in range(2):
                for tb in range(TB):
                    def q(h, tb=tb, hg=hg):
                        h = hg * NH + h
                        return [qnT[:, h, tb * P:(tb + 1) * P], qpe[:, h // 2, tb * P:(tb + 1) * P]]

                    def k(h, tb=tb, hg=hg):
                        h = hg * NH + h
                        return [knT[:, h, 0:(tb + 1) * P], kpe[:, h % 2, 0:(tb + 1) * P]]

                    def v(h, kb, hg=hg):
                        h = hg * NH + h
                        return mv_v[:, kb, h * P:(h + 1) * P]

                    def bias(h0, h1, tb=tb):
                        m = mtab[:, P:2 * P] if tb == 0 else mtab[:, 0:S]
                        return m.unsqueeze(1).to_broadcast([P, h1 - h0, (tb + 1) * P])

                    where = {"psum": lambda bank, h: bank[:, h * P:(h + 1) * P],
                             "out": lambda x, bank, tb=tb, hg=hg: (x[:, hg * NH:(hg + 1) * NH, tb * P:(tb + 1) * P],
                                                                   bank[:].rearrange("p (h q) -> p h q", h=NH))}
                    out.append(add_group(Group(tb, q, k, v, (P + ROPE) ** -0.5, bias, None, where, 2)))
            return out

        def mla_loads(pool, n):
            if n > 1:
                pool.wait_ge(x_done, 4 * (n - 1))
            pool.dma_start(mtab, I["table"][:, T_MLA:T_MLA + S + 2]).then_inc(m_in, 16)
            pool.dma_start(posi, I["positions_2"][0].partition_broadcast(P)).then_inc(m_in, 16)

        def mla_pool(pool, n):
            norm_pool(pool, n)
            for c, (sq, width) in enumerate(((2, 256), (6, 384))):
                pool.wait_ge(m_sq, sq)
                if c == 0:
                    src = lst[:, 0:2]
                else:
                    nc.gpsimd.tensor_tensor(lst[:, 6:8], lst[:, 2:4], lst[:, 4:6], ALU.add).then_inc(m_p1, 1)
                    pool.wait_ge(m_p1, 2)
                    src = lst[:, 6:8]
                nc.gpsimd.tensor_scalar(lst[:, 8 + 2 * c:10 + 2 * c], src, 1.0 / width, EPS, ALU.mult, ALU.add).then_inc(m_p1, 1)
                pool.wait_ge(m_p1, 1 + 2 * c)
                nc.gpsimd.tensor_tensor(lst[:, 12 + 2 * c:14 + 2 * c], lst[:, 8 + 2 * c:10 + 2 * c], mhalf[:, 0:2],
                                        ALU.pow).then_inc(m_rs, 1)

        def mla_pe(pe, n, ready, ready2, gs):
            u0 = first_unit["mla"]
            pe.wait_ge(lo_ready, u0 + 1)
            w = weights(u0, KT)
            for tb in range(TB):
                mm = tokens(W[0][:, tb * 256:(tb + 1) * 256], w, slice(0, 256), HT, KT, tb, ready if tb == 0 else None)
            mm.then_inc(unit_used, 1)
            pe.wait_ge(lo_ready, u0 + 2)
            up(W[1], u0 + 1)
            for k, width in enumerate((256, 128)):
                pe.wait_ge(lo_ready, u0 + 3 + k)
                w = weights(u0 + 2 + k, KT)
                for tb in range(TB):
                    mm = tokens(W[2 + k][:, tb * width:(tb + 1) * width], w, slice(0, width), HT, KT, tb,
                                ready2 if k == tb == 0 else None)
                mm.then_inc(unit_used, 1)
            pe.wait_ge(m_cn, 2)
            for t in range(2):
                for tb in range(TB):
                    tr = pe.transpose(W[0][:, t * S + tb * P:t * S + (tb + 1) * P], cn[:, tb, t * P:(t + 1) * P], ident[:])
            tr.then_inc(m_ct, 1)
            for g in range(2):
                u = u0 + 4 + g
                if g == 1:
                    pe.wait_ge(m_cn, 6)
                    for t in range(3):
                        for tb in range(TB):
                            tr = pe.transpose(W[2 + t // 2][:, t % 2 * S + tb * P:t % 2 * S + (tb + 1) * P],
                                              cqn[:, tb, t * P:(t + 1) * P], ident[:])
                    tr.then_inc(m_ct, 1)
                pe.wait_ge(lo_ready, u + 1)
                pe.wait_ge(m_cl, 2)
                if g == 0:
                    pe.wait_ge(n_lo, n_hi_count[n] + 16)
                else:
                    pe.wait_ge(m_ev, 4)
                w = weights(u, 2)
                for h in range(4):
                    features(ACC[h // 2][:, h % 2 * S:(h % 2 + 1) * S], w, slice(h * 256, h * 256 + P), cT, 2)
                wv = [x.rearrange("p k (h c) -> p k h c", h=4)[:, :, :, P:2 * P] for x in w]
                for tb in range(TB):
                    mm = tokens(ACC[2 + tb][:].rearrange("p (h c) -> p h c", h=4), wv, slice(None), cT, 2, tb)
                mm.then_inc(unit_used, 1)
            for g in range(4):
                u = u0 + 6 + g
                pe.wait_ge(lo_ready, u + 1)
                if g == 0:
                    pe.wait_ge(m_cl, 5)
                    pe.wait_ge(m_kp, 1)
                if g == 2:
                    pe.wait_ge(m_ev, 8)
                if g == 3:
                    pe.wait_ge(m_ev, 10)
                    pe.wait_ge(m_rq, 2)
                    pe.wait_ge(m_kz, 2)
                    for gr in gs[:2]:
                        at_scores(pe, gr)
                w = weights(u, 3)
                b0, b1 = (W[0], W[1], W[2], W[3], ACC[0], ACC[1], ACC[2], ACC[3])[2 * g:2 * g + 2]
                for h in range(2):
                    features(b0[:, h * S:(h + 1) * S], w, slice(h * P, (h + 1) * P), cqT, 3)
                features(b1[:, 0:S], w, slice(256, 384), cqT, 3)
                features(b1[:, S:2 * S], w, slice(384, 512), cqT, 3).then_inc(unit_used, 1)
            pe.wait_ge(m_ev, 11)
            pe.wait_ge(m_rq, 3)
            at_turn(pe, gs[0])
            pe.wait_ge(m_ev, 12)
            pe.wait_ge(m_rq, 4)
            attend_pe(pe, gs)
            pe.wait_ge(a_ol, gs[-1].g + 1)
            for r in range(4):
                pe.wait_ge(lo_ready, u0 + 11 + r)
                down(u0 + 10 + r, [x[:, 2 * r:2 * r + 2, :] for x in HT], first=r == 0, last=r == 3)

        def mla_act(act, n, gs):
            u0 = first_unit["mla"]
            sq = act_tmp[:].rearrange("p a (b c) -> p (a b) c", c=256)
            act.wait_ge(unit_used, u0 + 1)
            for tb in range(TB):
                nc.scalar.activation(sq[:, tb, :], W[0][:, tb * 256:(tb + 1) * 256], ACT.Square,
                                     accum_out=lst[:, tb:tb + 1]).then_inc(m_sq, 1)
            split_hi(act, u0 + 3)
            act.wait_ge(unit_used, u0 + 2)
            norm_hi(act, n, G_MIX2 + 8, 1)
            split_hi(act, u0 + 4)
            act.wait_ge(unit_used, u0 + 3)
            for tb in range(TB):
                nc.scalar.activation(sq[:, 2 + tb, :], W[2][:, tb * 256:(tb + 1) * 256], ACT.Square,
                                     accum_out=lst[:, 2 + tb:3 + tb]).then_inc(m_sq, 1)
            split_hi(act, u0 + 5)
            act.wait_ge(unit_used, u0 + 4)
            for tb in range(TB):
                nc.scalar.activation(sq[:, 4 + tb, 0:128], W[3][:, tb * 128:(tb + 1) * 128], ACT.Square,
                                     accum_out=lst[:, 4 + tb:5 + tb]).then_inc(m_sq, 1)
            act.wait_ge(m_ct, 1)
            for t in range(2):
                nc.scalar.mul(cT[0][:, t, :], W[0][:, t * S:(t + 1) * S], par[:, G_KV + t:G_KV + t + 1]).then_inc(m_ch2, 1)
            split_hi(act, u0 + 6)
            act.wait_ge(m_ct, 2)
            for t in range(3):
                nc.scalar.mul(cqT[0][:, t, :], W[2 + t // 2][:, t % 2 * S:(t % 2 + 1) * S],
                              par[:, G_Q + t:G_Q + t + 1]).then_inc(m_ch2, 1)
            for g in range(2):
                act.wait_ge(unit_used, u0 + 5 + g)
                for b in range(2):
                    nc.scalar.copy(knT[:, 4 * g + 2 * b:4 * g + 2 * b + 2, :],
                                   ACC[b][:].rearrange("p (h s) -> p h s", h=2)).then_inc(m_ev, 1)
                for tb in range(TB):
                    nc.scalar.copy(mv_v[:, tb, g * 512:(g + 1) * 512], ACC[2 + tb][:]).then_inc(m_ev, 1)
                split_hi(act, u0 + 7 + g)
            for g in range(4):
                act.wait_ge(unit_used, u0 + 7 + g)
                b0 = (W[0], W[2], ACC[0], ACC[2])[g]
                nc.scalar.copy(qnT[:, 2 * g:2 * g + 2, :], b0[:].rearrange("p (h s) -> p h s", h=2)).then_inc(m_ev, 1)
                if g < 2:
                    split_hi(act, u0 + 9 + g)
                if g == 2:
                    at_exp(act, gs[0])
                    at_exp(act, gs[1])
            attend_act(act, gs, lambda k: split_hi(act, u0 + 11 + k))
            for r in range(3):
                split_hi(act, u0 + 13 + r)

        mpairs = 16

        def angles_dve(dve, j):
            sgn, inv = mtab[:, S + 1:S + 2], mtab[:, S:S + 1]

            def left(r, k, quarter):
                return [lambda: nc.vector.scalar_tensor_tensor(r, k, -C1, ang, ALU.mult, ALU.add),
                        lambda: nc.vector.scalar_tensor_tensor(r, k, -C2, r, ALU.mult, ALU.add),
                        lambda: nc.vector.scalar_tensor_tensor(r, k, -C3, r, ALU.mult, ALU.add),
                        lambda: nc.vector.tensor_scalar(r, r, quarter, 3.1415925, ALU.add, ALU.min),
                        lambda: nc.vector.tensor_scalar(r, r, -3.1415925, None, ALU.max)]

            steps = [lambda: nc.vector.tensor_copy(mpos, posi),
                     lambda: nc.vector.tensor_scalar(ang, mpos, inv, None, ALU.mult),
                     lambda: nc.vector.tensor_scalar(kt_, ang, 1.0 / TWO_PI, None, ALU.mult),
                     lambda: nc.vector.tensor_scalar(kc_, kt_, 0.25, MAGIC, ALU.add, ALU.add),
                     lambda: nc.vector.tensor_scalar(kt_, kt_, MAGIC, None, ALU.add),
                     lambda: nc.vector.tensor_scalar(kt_, kt_, MAGIC, None, ALU.subtract),
                     lambda: nc.vector.tensor_scalar(kc_, kc_, MAGIC, None, ALU.subtract)]
            steps += left(r1, kt_, 0.0) + left(r2, kc_, TWO_PI / 4)
            cuts = {0: (0, 6), 1: (6, 12), mpairs - 2: (12, 17)}
            if j == 0:
                dve.wait_ge(m_in, 32)
            if j in cuts:
                for k in range(*cuts[j]):
                    if k:
                        dve.wait_ge(m_ch, k)
                    steps[k]().then_inc(m_ch, 1)
            if j == mpairs - 1:
                dve.wait_ge(m_cs, 2)
                nc.vector.tensor_scalar(sinT, sinT, sgn, None, ALU.mult).then_inc(m_ch, 1)

        def angles_act(act, j):
            if j == mpairs - 2:
                act.wait_ge(m_ch, 17)
                nc.scalar.activation(sinT, r1, ACT.Sin).then_inc(m_cs, 1)
                nc.scalar.activation(cosT, r2, ACT.Sin).then_inc(m_cs, 1)

        def mla_dve(dve, n, gs):
            u0 = first_unit["mla"]
            def rope(dsts, bank, k, done):
                a, b = ropet[:, 2 * (k % 2), :], ropet[:, 2 * (k % 2) + 1, :]
                nc.vector.tensor_tensor(a, bank[:, 0:S], cosT, ALU.mult).then_inc(m_rp, 1)
                nc.vector.tensor_tensor(b, bank[:, S:2 * S], sinT, ALU.mult).then_inc(m_rp, 1)
                dve.wait_ge(m_rp, 2 * k + 2)
                for r, dst in dsts:
                    last = nc.vector.tensor_tensor(dst, a[r], b[r], ALU.add)
                last.then_inc(done, 1)

            nc.vector.memset(kpe[ROPE:P, 0, :], 0.0).then_inc(m_kz, 1)
            nc.vector.memset(kpe[0:ROPE, 1, :], 0.0).then_inc(m_kz, 1)
            dve.wait_ge(m_ch, 18)
            dve.wait_ge(m_rs, 1)
            for tb in range(TB):
                nc.vector.tensor_scalar(cn[:, tb, :], W[0][:, tb * 256:(tb + 1) * 256], lst[:, 12 + tb:13 + tb], None,
                                        ALU.mult).then_inc(m_cn, 1)
            split_lo(dve, u0 + 3)
            norm_lo(dve, n, G_MIX2 + 8, 1)
            rope([(slice(0, ROPE), kpe[0:ROPE, 0, :]), (slice(ROPE, P), kpe[ROPE:P, 1, :])], W[1], 0, m_kp)
            split_lo(dve, u0 + 4)
            split_lo(dve, u0 + 5)
            dve.wait_ge(m_ch2, 2)
            for t in range(2):
                nc.vector.scalar_tensor_tensor(cT[1][:, t, :], W[0][:, t * S:(t + 1) * S], par[:, G_KV + t:G_KV + t + 1],
                                               cT[0][:, t, :].bitcast(F32), ALU.mult, ALU.subtract).then_inc(m_cl, 1)
            dve.wait_ge(m_rs, 2)
            for tb in range(TB):
                nc.vector.tensor_scalar(cqn[:, tb, 0:256], W[2][:, tb * 256:(tb + 1) * 256], lst[:, 14 + tb:15 + tb], None,
                                        ALU.mult).then_inc(m_cn, 1)
                nc.vector.tensor_scalar(cqn[:, tb, 256:384], W[3][:, tb * 128:(tb + 1) * 128], lst[:, 14 + tb:15 + tb],
                                        None, ALU.mult).then_inc(m_cn, 1)
            split_lo(dve, u0 + 6)
            for t in range(3):
                dve.wait_ge(m_ch2, 5)
                nc.vector.scalar_tensor_tensor(cqT[1][:, t, :], W[2 + t // 2][:, t % 2 * S:(t % 2 + 1) * S],
                                               par[:, G_Q + t:G_Q + t + 1], cqT[0][:, t, :].bitcast(F32), ALU.mult,
                                               ALU.subtract).then_inc(m_cl, 1)
            for g in range(2):
                split_lo(dve, u0 + 7 + g)
            for g in range(4):
                dve.wait_ge(unit_used, u0 + 7 + g)
                rope([(slice(0, P), qpe[:, g, :])], (W[1], W[3], ACC[1], ACC[3])[g], 1 + g, m_rq)
                if g < 2:
                    split_lo(dve, u0 + 9 + g)
                if g == 2:
                    at_max(dve, gs[0])
                    at_max(dve, gs[1])
                    at_norm(dve, gs[0])
            attend_dve(dve, gs, lambda k: split_lo(dve, u0 + 11 + k))
            for r in range(2):
                split_lo(dve, u0 + 13 + r)

        cut = cutter()
        qaT = cut(2, S)
        kaZ = cut(2, S)
        va = cut(TB, P)
        qbT = cut(2, S)
        kbZ = cut(NH, S)
        vb = cut(TB, S)
        qT, kT, vT = cut(NH, S), cut(NH, S), cut(NH, S)
        zs = cut(TB, NH * DN)
        ktok, vtok = cut(G8, P), cut(G8, P)
        Lm, Om, Em, Dm, At = (cut(G8, P) for _ in range(5))
        kbg = cut(G8, P)
        msk = cut(10, P)
        EM = Ym = ktok
        kdec = vT.rearrange("p h s -> p (h s)").rearrange("p (g d) -> p g d", g=G8)
        qdt = At
        un, wTm, vnew, orow = Dm, Om, kbg, Lm
        oT = Em.rearrange("p g e -> p (g e)").rearrange("p (t s) -> p t s", s=S)
        St = act_tmp[:, 0, :].rearrange("p (h e) -> p h e", h=NH)
        alibi = XN[:].rearrange("p a b -> p (a b)").rearrange("p (k h s) -> p k h s", k=2, h=NH)
        dd = sb("dd", [P, 260])
        dnr = sb("dnr", [P, DN])
        at_dd = [0]

        def small(*shape):
            n = math.prod(shape)
            v = dd[:, at_dd[0]:at_dd[0] + n]
            at_dd[0] += n
            return v.rearrange("p (a b) -> p a b", a=shape[0]) if len(shape) > 1 else v

        sinkb, alog, dtb = small(NH), small(NH), small(NH)
        ba = small(TB, 8)
        tt, ab, e1, e2, l2, be1, beta, spl, graw = (small(TB, NH) for _ in range(9))
        ea = small(NH)
        gcl = small(2, G8)
        eg, egd, egl, bg, qs, rq = (small(G8) for _ in range(6))
        ss, sse, ri = small(16), small(16), small(16)
        egS = small(G8, 2)
        oss, ose, ori = small(G8), small(G8), small(G8)

        d_zs = sem("d_zs")
        a_split = sem("a_split")
        d_in, d_al, d_z = sem("d_in"), sem("d_al"), sem("d_z")
        d_t, d_c, d_si, d_e = sem("d_t"), sem("d_c"), sem("d_si"), sem("d_e")
        d_ab, d_ex, d_ln, d_gc = sem("d_ab"), sem("d_ex"), sem("d_ln"), sem("d_gc")
        d_g, d_gm, d_gr = sem("d_g"), sem("d_gm"), sem("d_gr")
        d_tr, d_sq, d_ss, d_se, d_ri, d_x8 = (sem(f"d_{x}") for x in ("tr", "sq", "ss", "se", "ri", "x8"))
        d_kt, d_kq, d_t2, d_kn = sem("d_kt"), sem("d_kq"), sem("d_t2"), sem("d_kn")
        d_gg, d_di, d_ed, d_em = sem("d_gg"), sem("d_di"), sem("d_ed"), sem("d_em")
        d_gl, d_es, d_kd, d_ch = sem("d_gl"), sem("d_es"), sem("d_kd"), sem("d_ch")
        d_kk, d_la, d_at, d_ac = sem("d_kk"), sem("d_la"), sem("d_at"), sem("d_ac")
        v_o, v_y, v_yc, v_e, v_u = (sem(f"v_{x}") for x in ("o", "y", "yc", "e", "u"))
        u_p, u_c = sem("u_p"), sem("u_c")
        c_w, c_v, c_k, c_s, c_o = (sem(f"c_{x}") for x in ("w", "v", "k", "s", "o"))
        f_sq, f_ss, f_se, f_ri, f_o, f_tr, f_hi, f_lo, f_zd = (sem(f"f_{x}") for x in ("sq", "ss", "se", "ri", "o", "tr", "hi", "lo", "zd"))

        def four(bank):
            return bank[:].rearrange("p (h e) -> p h e", h=NH)

        def per_head(x, tb, n=P):
            return x[:, tb * NH:(tb + 1) * NH].unsqueeze(2).to_broadcast([P, NH, n])

        def gs_(tb):
            return slice(tb * NH, (tb + 1) * NH)

        def mix_groups():
            out = []
            for kind in range(2):
                for tb in range(TB):
                    def q(h, tb=tb, kind=kind):
                        t = h // 2 if kind else h % 2
                        return [(qbT if kind else qaT)[:, t, tb * P:(tb + 1) * P]]

                    def k(h, tb=tb, kind=kind):
                        return [(kbZ[:, h, 0:(tb + 1) * P] if kind else kaZ[:, h // 2, 0:(tb + 1) * P])]

                    def v(h, kb, kind=kind):
                        return vb[:, kb, h * HD:(h + 1) * HD] if kind else va[:, kb, h // 2 * HD:(h // 2 + 1) * HD]

                    def bias(h0, h1, tb=tb, kind=kind):
                        return alibi[:, kind, h0:h1, (1 - tb) * P:S]

                    where = {"psum": lambda bank, h: bank[h % 2 * HD:(h % 2 + 1) * HD, h // 2 * P:(h // 2 + 1) * P],
                             "out": lambda x, bank, tb=tb, kind=kind: (x[:, 2 * kind:2 * kind + 2, tb * P:(tb + 1) * P],
                                                                       bank[:, 0:S].rearrange("p (t q) -> p t q", t=2))}
                    out.append(add_group(Group(tb, q, k, v, HD ** -0.5, bias, None if kind else sinkb, where, 1)))
            return out

        B = ps[2:] + ps[:2]

        def slot_pe(pe, s, gs):
            for k, step in ((s - 2, at_out), (s - 1, at_turn), (s, at_scores)):
                if 0 <= k < len(gs):
                    step(pe, gs[k])

        def slot_act(act, s, gs):
            if 0 <= s - 3 < len(gs):
                at_keep(act, gs[s - 3], oT)
            if 0 <= s - 2 < len(gs):
                at_copy(act, gs[s - 2])
            if 0 <= s - 1 < len(gs):
                at_exp(act, gs[s - 1])

        def slot_dve(dve, s, gs):
            if 0 <= s - 1 < len(gs):
                at_max(dve, gs[s - 1])
                at_norm(dve, gs[s - 1])

        def mix_pool(pool, n):
            pool.dma_start(msk, I["table"][:, T_TRI:T_MLA].rearrange("p (a b) -> p a b", b=P)).then_inc(d_in, 16)
            pool.dma_start(sinkb, I["swa_sinks"][0].partition_broadcast(P)).then_inc(d_in, 16)
            pool.dma_start(alog, I["dn_a_log"][0].partition_broadcast(P)).then_inc(d_in, 16)
            pool.dma_start(dtb, I["dn_dt_bias"][0].partition_broadcast(P)).then_inc(d_in, 16)
            pool.dma_start(dnr[:], I["dn_norm"][0].partition_broadcast(P)).then_inc(d_in, 16)
            norm_pool(pool, n)
            pool.wait_ge(n_tr, 4 * n + 4)
            pool.dma_start(alibi, I["alibi"].rearrange("p (k h s) -> p k h s", k=2, h=NH)).then_inc(d_al, 16)
            for k in range(2):
                c = slice(k * G8, (k + 1) * G8)
                pool.wait_ge(d_ss, 2 * k + 2)
                nc.gpsimd.tensor_scalar(sse[:, c], ss[:, c], EPS, None, ALU.add).then_inc(d_se, 1)
                pool.wait_ge(d_se, k + 1)
                nc.gpsimd.tensor_tensor(ri[:, c], sse[:, c], mhalf[:, c], ALU.pow).then_inc(d_ri, 1)
            pool.wait_ge(d_la, 2)
            for lv in range(LEVELS):
                for tb in range(TB):
                    if lv:
                        pool.wait_ge(v_y, 2 * (lv - 1) + tb + 1)
                    if lv == 1:
                        pool.wait_ge(v_u, 2 * tb + 2)
                    nc.gpsimd.tensor_tensor(Om[:, gs_(tb), :], Lm[:, gs_(tb), :],
                                            msk[:, 4 + lv, :].unsqueeze(1).to_broadcast([P, NH, P]), ALU.mult).then_inc(v_o, 1)
            pool.wait_ge(f_ss, 2)
            nc.gpsimd.tensor_scalar(ose, oss, 1.0 / DN, EPS, ALU.mult, ALU.add).then_inc(f_se, 1)
            pool.wait_ge(f_se, 1)
            nc.gpsimd.tensor_tensor(ori, ose, mhalf[:, 0:G8], ALU.pow).then_inc(f_ri, 1)

        def rows_pe(pe, k, x):
            if k == 2:
                pe.wait_ge(d_si, 6)
            for tb in range(TB):
                for h in range(NH):
                    tr = pe.transpose(B[2 * k + tb][:, h * P:(h + 1) * P], x[:, h, tb * P:(tb + 1) * P], ident[:])
                tr.then_inc(d_tr, 1)

        def mix_pe(pe, n, ready, gs):
            u0 = first_unit["mix"]
            for k in range(14):
                u = u0 + k
                pe.wait_ge(lo_ready, u + 1)
                if 2 <= k < 8:
                    pe.wait_ge(d_e, k - 1)
                elif k >= 8:
                    pe.wait_ge(d_c, 6 * (k - 7))
                bank, rd = W[k % 2], ready if k == 0 else None
                w = weights(u, KT)
                if k in (0, 1, 4) or 6 <= k < 12:
                    up(bank, u, rd)
                else:
                    c0, width = {5: (0, 8), 3: (P, P)}.get(k, (0, UC))
                    at = 0
                    if k == 3:
                        features(bank[:, 0:S], w, slice(0, P), HT, KT)
                        at = S
                    for tb in range(TB):
                        mm = tokens(bank[:, at + tb * width:at + (tb + 1) * width], w, slice(c0, c0 + width), HT, KT, tb)
                    mm.then_inc(unit_used, 1)
                if k == 3:
                    start_pe(pe)
                if k == 5:
                    pe.wait_ge(d_e, 5)
                    pe.wait_ge(d_z, 1)
                    pe.wait_ge(par_ok, 1)
                if k >= 5:
                    slot_pe(pe, k - 5, gs)
                if k == 11:
                    pe.wait_ge(d_si, 4)
                    rows_pe(pe, 0, kT)
                    rows_pe(pe, 1, qT)
            pe.wait_ge(a_ol, gs[-1].g + 1)
            rows_pe(pe, 2, vT)
            pe.wait_ge(d_g, 1)
            pe.wait_ge(d_in, 80)
            pe.wait_ge(d_e, 8)
            gr = graw.rearrange("p a b -> p (a b)")
            nc.tensor.matmul(B[6][:, 0:G8], msk[:, 0, :], gr, start=True, stop=True)
            nc.tensor.matmul(B[6][:, G8:2 * G8], msk[:, 1, :], gr, start=True, stop=True).then_inc(d_gm, 1)
            for tb in range(TB):
                if tb:
                    pe.wait_ge(d_gc, 1)
                for h in range(NH):
                    g = tb * NH + h
                    mm = nc.tensor.matmul(B[7 - tb][:, h * P:(h + 1) * P], gr[:, g:g + 1].to_broadcast([P, P]), msk[:, 0, :],
                                          start=True, stop=True)
                mm.then_inc(d_gr, 1)
            for tb in range(TB):
                pe.wait_ge(d_kt, tb + 1)
                for h in range(NH):
                    tr = pe.transpose(B[tb][:, h * P:(h + 1) * P], ktok[:, tb * NH + h, :], ident[:])
                tr.then_inc(d_t2, 1)
            pe.wait_ge(d_kq, 2)
            for tb in range(TB):
                pe.wait_ge(d_kn, tb + 1)
                pe.wait_ge(d_x8, 2 * tb + 2)
                for h in range(NH):
                    kn = kT[:, h, tb * P:(tb + 1) * P]
                    nc.tensor.matmul(B[tb][:, h * P:(h + 1) * P], kn, kn, start=True, stop=True)
                    mm = nc.tensor.matmul(B[4 + tb][:, h * P:(h + 1) * P], qT[:, h, tb * P:(tb + 1) * P], kn,
                                          start=True, stop=True)
                mm.then_inc(d_kk, 1)
            for tb in range(TB):
                for h in range(NH):
                    tr = pe.transpose(B[2 + tb][:, h * P:(h + 1) * P], qdt[:, tb * NH + h, :], ident[:])
                tr.then_inc(d_t2, 1)
            for tb in range(TB):
                pe.wait_ge(d_la, tb + 1)
                for h in range(NH):
                    tr = pe.transpose(B[4 + tb][:, h * P:(h + 1) * P], Dm[:, tb * NH + h, :], ident[:])
                tr.then_inc(d_at, 1)
            pe.wait_ge(d_kn, 4)
            for tb in range(TB):
                pe.wait_ge(v_o, tb + 1)
                for h in range(NH):
                    tr = pe.transpose(B[tb][:, h * P:(h + 1) * P], Om[:, tb * NH + h, :], ident[:])
                tr.then_inc(v_y, 1)
            for lv in range(1, LEVELS):
                for tb in range(TB):
                    pe.wait_ge(v_o, 2 * lv + tb + 1)
                    pe.wait_ge(v_u, 4 * (lv - 1) + 2 * tb + 2)
                    for h in range(NH):
                        g = tb * NH + h
                        mm = nc.tensor.matmul(B[tb][:, h * P:(h + 1) * P], Om[:, g, :], Em[:, g, :], start=True, stop=True)
                    mm.then_inc(v_y, 1)
                for tb in range(TB):
                    pe.wait_ge(v_yc, 2 * (lv - 1) + tb + 1)
                    for h in range(NH):
                        g = tb * NH + h
                        mm = nc.tensor.matmul(B[2 + tb][:, h * P:(h + 1) * P], Dm[:, g, :], Ym[:, g, :], start=True, stop=True)
                    mm.then_inc(v_e, 1)
                    if lv < LEVELS - 1:
                        for h in range(NH):
                            g = tb * NH + h
                            mm = nc.tensor.matmul(B[6 + tb][:, h * P:(h + 1) * P], Ym[:, g, :], Dm[:, g, :], start=True,
                                                  stop=True)
                        mm.then_inc(v_e, 1)
            for tb in range(TB):
                pe.wait_ge(v_u, 4 * (LEVELS - 1) + tb + 1)
                for h in range(NH):
                    g = tb * NH + h
                    mm = nc.tensor.matmul(B[tb][:, h * P:(h + 1) * P], Em[:, g, :], vtok[:, g, :], start=True, stop=True)
                mm.then_inc(u_p, 1)
                for h in range(NH):
                    g = tb * NH + h
                    mm = nc.tensor.matmul(B[2 + tb][:, h * P:(h + 1) * P], kbg[:, g, :], Em[:, g, :], start=True, stop=True)
                mm.then_inc(u_p, 1)
            for c in range(2 * TB):
                tb, r = c // 2, c % 2 * CH
                rr = slice(r, r + CH)
                if c % 2 == 0:
                    pe.wait_ge(u_c, 2 * tb + 2)
                pe.wait_ge(c_s, c + 1)
                for h in range(NH):
                    mm = nc.tensor.matmul(B[4][rr, h * P:(h + 1) * P], wTm[:, tb * NH + h, rr], St[:, h, :], start=True,
                                          stop=True)
                mm.then_inc(c_w, 1)
                for h in range(NH):
                    nc.tensor.matmul(B[6 + tb][rr, h * P:(h + 1) * P], qT[:, h, tb * P + r:tb * P + r + CH], St[:, h, :],
                                     start=h == 0, stop=False, skip_group_check=True)
                pe.wait_ge(c_v, c + 1)
                if c < 3:
                    for h in range(NH):
                        mm = nc.tensor.matmul(B[5][:, h * P:(h + 1) * P], kdec[rr, tb * NH + h, :],
                                              vnew[rr, tb * NH + h, :], start=True, stop=True)
                    mm.then_inc(c_k, 1)
                if c % 2:
                    for h in range(NH):
                        mm = nc.tensor.matmul(B[6 + tb][:, h * P:(h + 1) * P], At[:, tb * NH + h, :],
                                              vnew[:, tb * NH + h, :], start=False, stop=True, skip_group_check=True)
                    mm.then_inc(c_o, 1)
            pe.wait_ge(a_split, 2)
            for r in range(2):
                pe.wait_ge(lo_ready, u0 + 15 + r)
                down(u0 + 14 + r, [x[:, 2 * r:2 * r + 2, :] for x in HT], first=r == 0)
            for tb in range(TB):
                pe.wait_ge(f_o, 2 * tb + 2)
                for h in range(NH):
                    tr = pe.transpose(B[tb][:, h * P:(h + 1) * P], orow[:, tb * NH + h, :], ident[:])
                tr.then_inc(f_tr, 1)
            pe.wait_ge(f_lo, 2)
            for r in range(2, 4):
                pe.wait_ge(lo_ready, u0 + 15 + r)
                down(u0 + 14 + r, [x[:, 2 * r:2 * r + 2, :] for x in HT], last=r == 3)

        def mix_act(act, n, gs):
            u0 = first_unit["mix"]
            dst = (qT, kT, vT)

            def silu(k):
                act.wait_ge(d_c, 6 * k + 6)
                x = dst[k // 2][:, k % 2 * 2:k % 2 * 2 + 2, :]
                nc.scalar.activation(x, x, ACT.Silu).then_inc(d_si, 1)

            for k in range(14):
                act.wait_ge(unit_used, u0 + k + 1)
                bank = W[k % 2]
                if k in (0, 4):
                    nc.scalar.copy(qaT if k else qbT, bank[:].rearrange("p (t s) -> p t s", t=2)).then_inc(d_e, 1)
                elif k == 3:
                    nc.scalar.copy(kaZ[0:HD, 0, :], bank[0:HD, 0:S])
                    nc.scalar.copy(kaZ[HD:P, 1, :], bank[HD:P, 0:S])
                    nc.scalar.copy(va, bank[:, S:2 * S].rearrange("p (b c) -> p b c", b=TB)).then_inc(d_e, 1)
                elif k == 1:
                    act.wait_ge(d_z, 1)
                    kz = kbZ.rearrange("p (t e) s -> p t e s", e=2)
                    for e in range(2):
                        hs = slice(e * HD, (e + 1) * HD)
                        last = nc.scalar.copy(kz[hs, :, e, :], bank[hs, :].rearrange("p (t s) -> p t s", t=2))
                    last.then_inc(d_e, 1)
                elif k == 2:
                    nc.scalar.copy(vb, bank[:].rearrange("p (b c) -> p b c", b=TB)).then_inc(d_e, 1)
                elif k > 11:
                    nc.scalar.copy(zs[:, :, (k - 12) * S:(k - 11) * S], bank[:].rearrange("p (b c) -> p b c", b=TB)).then_inc(d_e, 1)
                elif k == 5:
                    nc.scalar.copy(ba, bank[:, 0:16].rearrange("p (b c) -> p b c", b=TB)).then_inc(d_e, 1)
                else:
                    for t in range(PAIR):
                        c = CONV_D + 3 * 12 + 2 * (k - 6) + t
                        nc.scalar.mul(dst[(k - 6) // 2][:, (k - 6) % 2 * 2 + t, :], bank[:, t * S:(t + 1) * S],
                                      par[:, c:c + 1]).then_inc(d_t, 1)
                split_hi(act, u0 + k + 3)
                if k == 4:
                    start_act(act)
                for m in {9: (0, 1), 10: (2, 3), 11: (4,), 12: (5,)}.get(k, ()):
                    silu(m)
                if k == 12:
                    for m in range(4):
                        act.wait_ge(d_tr, m + 1)
                        nc.scalar.activation((Lm, Lm, Om, Om)[m][:, gs_(m % 2), :], four(B[m]), ACT.Square).then_inc(d_sq, 1)
                if 5 <= k < 13:
                    slot_act(act, k - 4, gs)
                if k == 8:
                    act.wait_ge(d_in, 80)
                    act.wait_ge(d_ab, 1)
                    nc.scalar.activation(e1, ba[:, :, 0:NH], ACT.Exp, scale=-1.0).then_inc(d_ex, 1)
                    nc.scalar.activation(e2, ab, ACT.Exp, scale=-1.0).then_inc(d_ex, 1)
                    nc.scalar.activation(ea, alog, ACT.Exp).then_inc(d_ex, 1)
                    act.wait_ge(d_ex, 2)
                    nc.scalar.activation(l2, e2, ACT.Ln, bias=1.0).then_inc(d_ln, 1)
            act.wait_ge(d_e, 8)
            nc.scalar.activation(zs, zs, ACT.Silu).then_inc(d_zs, 1)
            nc.scalar.copy(hT_hi[:, 0:4, :], oT).then_inc(a_split, 1)
            act.wait_ge(d_gm, 1)
            nc.scalar.copy(gcl.rearrange("p a b -> p (a b)"), B[6][:, 0:16]).then_inc(d_gc, 1)
            act.wait_ge(d_gc, 1)
            nc.scalar.activation(eg, gcl[:, 0, :], ACT.Exp).then_inc(d_gg, 1)
            act.wait_ge(d_gl, 1)
            nc.scalar.activation(egl, egd, ACT.Exp).then_inc(d_gg, 1)
            for tb in range(TB):
                act.wait_ge(d_gr, tb + 1)
                nc.scalar.activation(egS[:, gs_(tb), :], B[7 - tb][:, CH - 1::CH].rearrange("p (h c) -> p h c", h=NH),
                                     ACT.Exp).then_inc(d_es, 1)
            for tb in range(TB):
                act.wait_ge(d_t2, tb + 1)
                nc.scalar.copy(kT[:, :, tb * P:(tb + 1) * P], four(B[tb])).then_inc(d_kn, 1)
            for tb in range(TB):
                act.wait_ge(d_di, NH * (tb + 1))
                nc.scalar.activation(EM[:, gs_(tb), :], EM[:, gs_(tb), :], ACT.Exp).then_inc(d_ed, 1)
            for tb in range(TB):
                act.wait_ge(d_t2, 3 + tb)
                nc.scalar.copy(qT[:, :, tb * P:(tb + 1) * P], four(B[2 + tb])).then_inc(d_kn, 1)
            for tb in range(TB):
                act.wait_ge(d_at, tb + 1)
                nc.scalar.copy(At[:, gs_(tb), :], four(B[4 + tb])).then_inc(d_ac, 1)
            for lv in range(1, LEVELS):
                for tb in range(TB):
                    act.wait_ge(v_y, 2 * lv + tb + 1)
                    if lv > 1:
                        act.wait_ge(v_e, 4 * (lv - 2) + 2 * tb + 2)
                    nc.scalar.copy(Ym[:, gs_(tb), :], four(B[tb])).then_inc(v_yc, 1)
            for tb in range(TB):
                act.wait_ge(u_p, 2 * tb + 1)
                nc.scalar.copy(un[:, gs_(tb), :], four(B[tb])).then_inc(u_c, 1)
                act.wait_ge(u_p, 2 * tb + 2)
                nc.scalar.copy(wTm[:, gs_(tb), :], four(B[2 + tb])).then_inc(u_c, 1)
            for tb in range(TB):
                act.wait_ge(c_o, tb + 1)
                nc.scalar.activation(Ym[:, gs_(tb), :], four(B[6 + tb]), ACT.Square).then_inc(f_sq, 1)
            for tb in range(TB):
                act.wait_ge(f_tr, tb + 1)
                nc.scalar.copy(hT_hi[:, 4:8, tb * P:(tb + 1) * P], four(B[tb])).then_inc(f_hi, 1)
            for r in range(3):
                split_hi(act, u0 + 17 + r)

        def mix_dve(dve, n, gs):
            u0 = first_unit["mix"]
            nc.vector.memset(kaZ, 0.0)
            nc.vector.memset(kbZ, 0.0).then_inc(d_z, 1)

            def bc(x):
                return x.unsqueeze(1).to_broadcast([P, TB, NH])
            count = [0]

            def chained(ins):
                count[0] += 1
                ins.then_inc(d_ch, 1)
                dve.wait_ge(d_ch, count[0])

            for k in range(14):
                if 6 <= k < 12:
                    bank, m = W[k % 2], k - 6
                    dve.wait_ge(d_t, 2 * m + 2)
                    for back in (1, 2, 3):
                        for t in range(PAIR):
                            if back > 1:
                                dve.wait_ge(d_c, 6 * m + 2 * (back - 2) + t + 1)
                            c = CONV_D + (3 - back) * 12 + 2 * m + t
                            ys = (qT, kT, vT)[m // 2][:, m % 2 * 2 + t, back:S]
                            nc.vector.scalar_tensor_tensor(ys, bank[:, t * S:(t + 1) * S - back], par[:, c:c + 1], ys,
                                                           ALU.mult, ALU.add).then_inc(d_c, 1)
                split_lo(dve, u0 + k + 3)
                if k == 5:
                    dve.wait_ge(d_in, 80)
                    dve.wait_ge(d_al, 16)
                if k >= 5:
                    slot_dve(dve, k - 4, gs)
                if k == 5:
                    dve.wait_ge(d_e, 6)
                    chained(nc.vector.tensor_tensor(tt, ba[:, :, NH:8], bc(dtb), ALU.add))
                    nc.vector.scalar_tensor_tensor(ab, tt, -1.0, tt, ALU.mult, ALU.max).then_inc(d_ab, 1)
                elif k == 9:
                    dve.wait_ge(d_ex, 3)
                    chained(nc.vector.tensor_scalar(be1, e1, 1.0, None, ALU.add))
                    chained(nc.vector.reciprocal(beta, be1))
                    dve.wait_ge(d_ln, 1)
                    chained(nc.vector.scalar_tensor_tensor(spl, tt, 0.0, l2, ALU.max, ALU.add))
                    nc.vector.scalar_tensor_tensor(graw, spl, -1.0, bc(ea), ALU.mult, ALU.mult).then_inc(d_g, 1)
                if k == 12:
                    for m in range(4):
                        dve.wait_ge(d_sq, m + 1)
                        nc.vector.tensor_reduce(ss[:, 4 * m:4 * m + 4], (Lm, Lm, Om, Om)[m][:, gs_(m % 2), :], AX_X,
                                                ALU.add).then_inc(d_ss, 1)
            dve.wait_ge(a_split, 1)
            nc.vector.tensor_tensor(hT_lo[:, 0:4, :], oT, hT_hi[:, 0:4, :].bitcast(F32), ALU.subtract).then_inc(a_split, 1)
            dve.wait_ge(d_gc, 1)
            nc.vector.tensor_tensor(egd, gcl[:, 1, :], gcl[:, 0, :], ALU.subtract).then_inc(d_gl, 1)
            be = beta.rearrange("p a b -> p (a b)")
            dve.wait_ge(d_gg, 1)
            chained(nc.vector.tensor_tensor(bg, be, eg, ALU.mult))
            dve.wait_ge(d_ri, 1)
            for tb in range(TB):
                nc.vector.tensor_tensor(ktok[:, gs_(tb), :], four(B[tb]), per_head(ri, tb), ALU.mult).then_inc(d_kt, 1)
            dve.wait_ge(d_ri, 2)
            chained(nc.vector.tensor_scalar(rq, ri[:, 8:16], DN ** -0.5, None, ALU.mult))
            chained(nc.vector.tensor_tensor(qs, rq, eg, ALU.mult))
            for tb in range(TB):
                nc.vector.tensor_tensor(qdt[:, gs_(tb), :], four(B[2 + tb]), per_head(qs, tb), ALU.mult).then_inc(d_kq, 1)
            for tb in range(TB):
                dve.wait_ge(d_tr, 5 + tb)
                nc.vector.tensor_tensor(vtok[:, gs_(tb), :], four(B[4 + tb]), per_head(be, tb), ALU.mult).then_inc(d_x8, 1)
                dve.wait_ge(d_kt, tb + 1)
                nc.vector.tensor_tensor(kbg[:, gs_(tb), :], ktok[:, gs_(tb), :], per_head(bg, tb), ALU.mult).then_inc(d_x8, 1)
            dve.wait_ge(d_gg, 2)
            for tb in range(TB):
                nc.vector.tensor_tensor(kdec[:, gs_(tb), :], ktok[:, gs_(tb), :], per_head(egl, tb), ALU.mult).then_inc(d_kd, 1)
            dve.wait_ge(d_kd, 2)
            dve.wait_ge(d_es, 2)
            for tb in range(TB):
                dve.wait_ge(d_t2, tb + 1)
                for h in range(NH):
                    g = tb * NH + h
                    nc.vector.scalar_tensor_tensor(EM[:, g, :], B[7 - tb][:, h * P:(h + 1) * P], gcl[:, 0, g:g + 1],
                                                   msk[:, 2, :], ALU.subtract, ALU.mult).then_inc(d_di, 1)
            for tb in range(TB):
                dve.wait_ge(d_ed, tb + 1)
                nc.vector.tensor_tensor(EM[:, gs_(tb), :], EM[:, gs_(tb), :],
                                        msk[:, 3, :].unsqueeze(1).to_broadcast([P, NH, P]), ALU.mult).then_inc(d_em, 1)
            for tb in range(TB):
                dve.wait_ge(d_em, tb + 1)
                dve.wait_ge(d_kk, tb + 1)
                for h in range(NH):
                    g = tb * NH + h
                    hs = slice(h * P, (h + 1) * P)
                    nc.vector.scalar_tensor_tensor(Lm[:, g, :], B[tb][:, hs], be[:, g:g + 1], EM[:, g, :], ALU.mult,
                                                   ALU.mult)
                    last = nc.vector.scalar_tensor_tensor(Dm[:, g, :], B[4 + tb][:, hs], rq[:, g:g + 1], EM[:, g, :],
                                                          ALU.mult, ALU.mult)
                last.then_inc(d_la, 1)
            idb = ident[:].unsqueeze(1).to_broadcast([P, NH, P])
            for tb in range(TB):
                dve.wait_ge(v_y, tb + 1)
                nc.vector.tensor_tensor(Em[:, gs_(tb), :], idb, four(B[tb]), ALU.subtract).then_inc(v_u, 1)
                dve.wait_ge(d_at, tb + 1)
                nc.vector.tensor_tensor(Dm[:, gs_(tb), :], idb, Om[:, gs_(tb), :], ALU.subtract).then_inc(v_u, 1)
            dve.wait_ge(v_u, 4)
            for lv in range(1, LEVELS):
                for tb in range(TB):
                    two = lv < LEVELS - 1
                    for m, (x, b) in enumerate(((Em, 2), (Dm, 6)) if two else ((Em, 2),)):
                        dve.wait_ge(v_e, 4 * (lv - 1) + (2 * tb + 2 if two else tb + 1))
                        nc.vector.tensor_tensor(x[:, gs_(tb), :], x[:, gs_(tb), :], four(B[b + tb]),
                                                ALU.subtract).then_inc(v_u, 1)
            nc.vector.memset(St, 0.0).then_inc(c_s, 1)
            for c in range(2 * TB):
                tb, r = c // 2, c % 2 * CH
                rr = slice(r, r + CH)
                dve.wait_ge(c_w, c + 1)
                dve.wait_ge(u_c, 2 * tb + 1)
                nc.vector.tensor_tensor(vnew[rr, gs_(tb), :], un[rr, gs_(tb), :], four(B[4])[rr], ALU.subtract).then_inc(c_v, 1)
                if c < 3:
                    dve.wait_ge(c_k, c + 1)
                    for h in range(NH):
                        last = nc.vector.scalar_tensor_tensor(St[:, h, :], St[:, h, :], egS[:, tb * NH + h, c % 2:c % 2 + 1],
                                                              B[5][:, h * P:(h + 1) * P], ALU.mult, ALU.add)
                    last.then_inc(c_s, 1)
            for tb in range(TB):
                zt = zs[:, tb, :].rearrange("p (h e) -> p h e", h=NH)
                dve.wait_ge(d_zs, 1)
                nc.vector.tensor_tensor(zt, zt, dnr[:].unsqueeze(1).to_broadcast([P, NH, DN]), ALU.mult).then_inc(f_zd, 1)
            for tb in range(TB):
                dve.wait_ge(f_sq, tb + 1)
                nc.vector.tensor_reduce(oss[:, gs_(tb)], Ym[:, gs_(tb), :], AX_X, ALU.add).then_inc(f_ss, 1)
            dve.wait_ge(f_ri, 1)
            dve.wait_ge(f_zd, 2)
            for tb in range(TB):
                zt = zs[:, tb, :].rearrange("p (h e) -> p h e", h=NH)
                nc.vector.tensor_tensor(orow[:, gs_(tb), :], four(B[6 + tb]), per_head(ori, tb), ALU.mult).then_inc(f_o, 1)
                dve.wait_ge(f_o, 2 * tb + 1)
                nc.vector.tensor_tensor(orow[:, gs_(tb), :], orow[:, gs_(tb), :], zt, ALU.mult).then_inc(f_o, 1)
            for tb in range(TB):
                dve.wait_ge(f_hi, tb + 1)
                nc.vector.tensor_tensor(hT_lo[:, 4:8, tb * P:(tb + 1) * P], four(B[tb]),
                                        hT_hi[:, 4:8, tb * P:(tb + 1) * P].bitcast(F32), ALU.subtract).then_inc(f_lo, 1)
            for r in range(2):
                split_lo(dve, u0 + 17 + r)

        n_hi_count = [0]
        for st in stages:
            n_hi_count.append(n_hi_count[-1] + (16 if st == "mla" else 8))
        last_unit = {st: (first_unit[stages[k + 1]] if k + 1 < len(stages) else NU) - 1 for k, st in enumerate(stages)}
        gains = {"mix": G_MIX, "ffn": G_FFN, "gmlp": G_MIX2, "mlp0": G_MLP2, "mla": G_SRC, "mlp1": G_MLP2 + 8}
        passes = {}
        for st in stages:
            if st == "ffn":
                passes[st] = Pass(st, FT1 // PAIR, first_unit[st])
            elif st.startswith("mlp"):
                passes[st] = Pass(st, 16, first_unit[st])
            elif st == "gmlp":
                passes[st] = Pass(st, 8, first_unit[st] + 8)
        posts = [st for st in stages if st in ("mix", "ffn")]
        post_rows = {"mix": I["mix_post_norm"][0], "ffn": I["ffn_post_norm"][0]}
        N = len(stages)

        mix_gs = mix_groups() if "mix" in stages else []
        mla_gs = mla_groups() if "mla" in stages else []
        block = ctx.enter_context(nc.Block())

        @block.sync
        def _(sp):
            start_sync(sp)
            for n, st in enumerate(stages):
                if st == "ffn":
                    ffn_sync(sp, passes[st])
                elif st.startswith("mlp"):
                    mlp_sync(sp, passes[st], I["mlp_w1_2"][int(st[3])], I["mlp_w2_2"][int(st[3])])
                else:
                    for u in range(first_unit[st], last_unit[st] + 1):
                        load(sp, u)
                        if u == RAW - 1:
                            params_sync(sp)
            final_sync(sp)

        @block.gpsimd
        def _(pool):
            for n, st in enumerate(stages):
                if st in posts:
                    rows_load(pool, posts.index(st), post_rows[st])
                if st not in ("mix", "mla"):
                    norm_pool(pool, n)
                if st == "mix":
                    mix_pool(pool, n)
                elif st == "gmlp":
                    gmlp_pool(pool, n)
                elif st == "mla":
                    mla_pool(pool, n)
                if "gmlp" in stages[n + 1:n + 2]:
                    gmlp_loads(pool, n + 1)
                if "mla" in stages[n + 1:n + 2]:
                    mla_loads(pool, n + 1)
                if st in posts:
                    post_pool(pool, posts.index(st))
            rows_load(pool, len(posts), I["final_norm_g_2"])
            norm_pool(pool, N)

        @block.scalar
        def _(act):
            start_act_dmas(act)
            for n, st in enumerate(stages):
                norm_act(act, n, gains[st])
                if n:
                    split_hi(act, first_unit[st] + SPL - 1)
                else:
                    for u in range(1, SPL):
                        split_hi(act, u)
                if st == "mix":
                    mix_act(act, n, mix_gs)
                elif st == "ffn":
                    ffn_act(act, passes[st])
                elif st == "gmlp":
                    gmlp_act(act, n, passes[st])
                elif st == "mla":
                    mla_act(act, n, mla_gs)
                elif "mla" in stages[n + 1:n + 2]:
                    plain_act(act, passes[st], 3, ACT.Relu, angles_act)
                else:
                    plain_act(act, passes[st], 3, ACT.Relu)
                if st in posts:
                    post_act(act, n, last_unit[st])
            norm_act(act, N, None, False)

        @block.vector
        def _(dve):
            start_dve(dve)
            close = lambda b: None
            for n, st in enumerate(stages):
                norm_dve(dve, n, gains[st], close)
                if n:
                    for u in range(1, SPL):
                        split_lo(dve, first_unit[st] + u)
                else:
                    for u in range(1, SPL):
                        split_lo(dve, u)
                if st == "mix":
                    mix_dve(dve, n, mix_gs)
                elif st == "ffn":
                    ffn_dve(dve, passes[st])
                elif st == "gmlp":
                    gmlp_dve(dve, n, passes[st])
                elif st == "mla":
                    mla_dve(dve, n, mla_gs)
                elif "mla" in stages[n + 1:n + 2]:
                    plain_dve(dve, passes[st], 3, lambda j, m: act_tmp[:, m, :], angles_dve)
                else:
                    plain_dve(dve, passes[st], 3, lambda j, m: act_tmp[:, m, :])
                if st in posts:
                    close = post_dve(dve, posts.index(st))
                else:
                    close = res_dve(dve, n, last_unit[st])
            norm_dve(dve, N, None, close, False)
            final_dve(dve, N, len(posts))

        @block.tensor
        def _(pe):
            for n, st in enumerate(stages):
                if n == 0:
                    gain_pe(pe)
                    warm(pe, 6)
                elif stages[n - 1] in posts:
                    warm(pe, 20)
                norm_pe(pe, n, n and stages[n - 1] in posts)
                if n == 0:
                    warm(pe, 10)
                ready = h_ready(pe, n)
                if st == "mix":
                    mix_pe(pe, n, ready, mix_gs)
                elif st == "ffn":
                    ffn_pe(pe, passes[st], ready)
                elif st == "gmlp":
                    gmlp_pe(pe, n, passes[st], ready)
                elif st == "mla":
                    mla_pe(pe, n, ready, h_ready(pe, n, 1), mla_gs)
                else:
                    pe.wait_ge(lo_ready, first_unit[st] + 1)
                    up(W[0], first_unit[st], ready)
                    plain_pe(pe, passes[st], 3, ready)


def constants():
    import numpy as np

    i = np.arange(P)
    same = i[:, None] // CH == i[None, :] // CH
    low = same & (i[None, :] <= i[:, None])
    t = np.zeros((P, T_ALL), np.float32)
    t[:, T_ID:T_ID + P] = np.eye(P)
    t[:, T_TRI:T_TRI + P] = low.T
    t[:, T_BLK:T_BLK + P] = same
    t[:, T_NEG:T_NEG + P] = -1.0 * low
    t[:, T_LOW:T_LOW + P] = low
    for lv in range(LEVELS):
        b = 1 << lv
        r, c = i[:, None] // b, i[None, :] // b
        t[:, T_LEV + lv * P:T_LEV + (lv + 1) * P] = (r % 2 == 1) & (c == r - 1)
    q, k = i[:, None], np.arange(S)[None, :] - P
    t[:, T_MLA:T_MLA + S] = np.where(k // CH <= q // CH, 0.0, -1e30)
    f = np.arange(P) % (ROPE // 2)
    t[:, T_INV] = np.float32(10000.0) ** (-(2 * f).astype(np.float32) / np.float32(ROPE))
    t[:, T_SGN] = np.where(np.arange(P) // (ROPE // 2) % 2 == 0, -1.0, 1.0)
    slopes = 2.0 ** (-8.0 * np.arange(1, 2 * NH + 1) / (2 * NH))
    rel = (q - k).astype(np.float32)
    bias = np.zeros((P, 2, NH, S), np.float32)
    for kind in range(2):
        for h in range(NH):
            ok = (rel >= 0) & ((rel < 128) | (kind == 1))
            bias[:, kind, h] = np.where(ok, -np.float32(slopes[2 * h + kind]) * rel, -1e30)
    return {"table": t, "alibi": bias.reshape(P, -1)}


_INS = ['x', 'mix_pre_norm', 'w_in', 'swa_sinks', 'dn_conv_w', 'dn_a_log', 'dn_dt_bias', 'dn_norm', 'w_out',
        'mix_post_norm', 'ffn_pre_norm', 'w_up', 'ffn_conv_w', 'ffn_conv_b', 'w_down', 'ffn_post_norm',
        'positions_2', 'norm_mix_g_2', 'norm_mlp_g_2', 'a_w_in_2', 'a_ln_v_g_2', 'a_ln_v_b_2', 'a_w_s_2', 'a_b_s_2',
        'a_w_out_2', 'b_w_q_a_2', 'b_q_norm_g_2', 'b_w_q_b_2', 'b_w_o_2', 'kv_src_norm_g_2', 'kv_w_a_2',
        'kv_a_norm_g_2', 'kv_w_b_2', 'mlp_w1_2', 'mlp_w2_2', 'final_norm_g_2']


def kernel(**inputs):
    import numpy as _np
    import concourse.bacc as _bacc
    from concourse import mybir as _mybir
    from concourse.bass_utils import run_bass_kernel_spmd as _run

    nc = _bacc.Bacc("TRN2", target_bir_lowering=False, num_devices=1)
    arrays, views = {}, {}
    given = {name: _np.ascontiguousarray(inputs[name]) for name in _INS}
    for name, a in {**given, **constants()}.items():
        arrays[f"in_{name}_dram"] = a
        views[name] = nc.dram_tensor(f"in_{name}_dram", a.shape, _mybir.dt.from_np(a.dtype), kind="ExternalInput").ap()
    out = nc.dram_tensor("out_0_dram", (1, S, D), F32, kind="ExternalOutput").ap()
    build(nc, views, out, ("mix", "ffn", "gmlp", "mlp0", "mla", "mlp1"))
    r = _run(nc, [arrays], core_ids=[0])
    return r.results[0]["out_0_dram"]
```
